# Optimizing a Trainium2 kernel written in Bass

```python
import jax, jax.numpy as jnp
from jax import lax
import numpy as np

D_MODEL = 1024
BATCH = 1
SEQ = 1024
DEPTH = 2

GRID_W = 64
CTX_LEN = 256
CONV_DIM = 1024
CONV_WIDTH = 3
MLSTM_HEADS = 4
MLSTM_HEAD_DIM = 256
MLSTM_DIM = MLSTM_HEADS * MLSTM_HEAD_DIM
MLSTM_CHUNK = 64
MLSTM_K_SCALE = MLSTM_HEAD_DIM ** -0.5
NEG_INIT = -1e30
MLA_HEADS = 16
QK_NOPE_DIM = 128
QK_ROPE_DIM = 64
V_HEAD_DIM = 128
Q_LORA_RANK = 384
KV_LORA_RANK = 256
MLA_DIM = MLA_HEADS * V_HEAD_DIM
MLA_SCALE = (QK_NOPE_DIM + QK_ROPE_DIM) ** -0.5
ROPE_BASE = 10000.0
Q_BLOCK = 128
EVEN_IN_SIZES = (CONV_DIM, CONV_DIM, CONV_DIM, CONV_DIM, MLSTM_DIM, MLSTM_DIM, MLSTM_DIM, MLSTM_DIM, MLSTM_DIM, 4 * MLSTM_HEADS)
EVEN_IN_DIM = 4 * CONV_DIM + 5 * MLSTM_DIM + 4 * MLSTM_HEADS
EVEN_MIX_DIM = CONV_DIM + MLSTM_DIM
ODD_IN_SIZES = (Q_LORA_RANK, KV_LORA_RANK, QK_ROPE_DIM, MLA_DIM)
ODD_IN_DIM = Q_LORA_RANK + KV_LORA_RANK + QK_ROPE_DIM + MLA_DIM
N_EVEN = (DEPTH + 1) // 2
N_ODD = DEPTH // 2
LN_EPS = 1e-5
RMS_EPS = 1e-6
DEEPNORM_ALPHA = (2 * DEPTH) ** 0.25
DEEPNORM_BETA = (8 * DEPTH) ** -0.25

kernel_name = 'hybrid_conv_mlstm_mla_prefix_trunk'

def layer_norm(x, g, b):
    xf = x.astype(jnp.float32)
    mu = jnp.mean(xf, axis=-1, keepdims=True)
    var = jnp.mean(jnp.square(xf - mu), axis=-1, keepdims=True)
    return ((xf - mu) * lax.rsqrt(var + LN_EPS) * g + b).astype(x.dtype)

def rms_norm(x, g):
    xf = x.astype(jnp.float32)
    return (xf * lax.rsqrt(jnp.mean(jnp.square(xf), axis=-1, keepdims=True) + RMS_EPS) * g).astype(x.dtype)

def split_cols(p, sizes):
    out, start = [], 0
    for s in sizes:
        out.append(p[..., start:start + s])
        start += s
    return out

def axial_rope_tables(n_lat):
    rows = n_lat // GRID_W
    row = jnp.repeat(jnp.arange(rows, dtype=jnp.float32), GRID_W)
    col = jnp.tile(jnp.arange(GRID_W, dtype=jnp.float32), rows)
    n_freq = QK_ROPE_DIM // 4
    inv_freq = ROPE_BASE ** (-jnp.arange(n_freq, dtype=jnp.float32) / n_freq)
    ang = jnp.concatenate([row[:, None] * inv_freq, col[:, None] * inv_freq], axis=-1)
    return jnp.cos(ang), jnp.sin(ang)

def apply_rope(x, cos, sin):
    half = QK_ROPE_DIM // 2
    x1, x2 = x[..., :half], x[..., half:]
    return jnp.concatenate([x1 * cos - x2 * sin, x1 * sin + x2 * cos], axis=-1).astype(x.dtype)

def short_conv3(u, w):
    up = jnp.pad(u, ((0, 0), (1, 1), (0, 0)))
    return up[:, :-2] * w[0] + up[:, 1:-1] * w[1] + up[:, 2:] * w[2]

def mlstm_zero_state(bsz):
    return (jnp.zeros((bsz, MLSTM_HEADS, MLSTM_HEAD_DIM, MLSTM_HEAD_DIM), jnp.float32),
            jnp.zeros((bsz, MLSTM_HEADS, MLSTM_HEAD_DIM), jnp.float32),
            jnp.full((bsz, MLSTM_HEADS), NEG_INIT, jnp.float32))

def mlstm_chunkwise(q, k, v, i_pre, log_f, state):
    bsz, nh, t_len, dh = q.shape
    n_chunk = t_len // MLSTM_CHUNK

    def chunks(a):
        a = a.astype(jnp.float32).reshape((bsz, nh, n_chunk, MLSTM_CHUNK) + a.shape[3:])
        return jnp.moveaxis(a, 2, 0)

    xs = (chunks(q), chunks(k), chunks(v), chunks(i_pre), chunks(log_f))
    lower = jnp.tril(jnp.ones((MLSTM_CHUNK, MLSTM_CHUNK), dtype=bool))

    def step(carry, inp):
        c_st, n_st, m_st = carry
        qc, kc, vc, ic, fc = inp
        b = lax.cumsum(fc, axis=2)
        d = jnp.where(lower, b[..., :, None] - b[..., None, :] + ic[..., None, :], -jnp.inf)
        inter = b + m_st[..., None]
        m_t = jnp.maximum(inter, jnp.max(d, axis=-1))
        w = jnp.exp(d - m_t[..., None])
        a_inter = jnp.exp(inter - m_t)
        s = jnp.einsum('bhtd,bhsd->bhts', qc, kc) * w
        num = jnp.einsum('bhts,bhsd->bhtd', s, vc) + a_inter[..., None] * jnp.einsum('bhtk,bhkd->bhtd', qc, c_st)
        den = jnp.sum(s, axis=-1) + a_inter * jnp.einsum('bhtk,bhk->bht', qc, n_st)
        h = num / jnp.maximum(jnp.abs(den), jnp.exp(-m_t))[..., None]
        m_new = m_t[..., -1]
        decay = jnp.exp(b[..., -1] + m_st - m_new)
        w_tok = jnp.exp(b[..., -1:] - b + ic - m_new[..., None])
        kw = kc * w_tok[..., None]
        c_new = decay[..., None, None] * c_st + jnp.einsum('bhsk,bhsd->bhkd', kw, vc)
        n_new = decay[..., None] * n_st + jnp.sum(kw, axis=2)
        return (c_new, n_new, m_new), h

    state, hs = lax.scan(step, state, xs)
    return jnp.moveaxis(hs, 0, 2).reshape(bsz, nh, t_len, dh), state

def even_mixer(u_ctx, u_lat, w_in, conv_w, gate_b, w_out, need_ctx):
    s_ctx = split_cols(u_ctx @ w_in, EVEN_IN_SIZES)
    s_lat = split_cols(u_lat @ w_in, EVEN_IN_SIZES)

    def conv_branch(s):
        a_b, a_c, a_x, a_z = s[:4]
        return a_b * short_conv3(a_c * a_x, conv_w) * jax.nn.silu(a_z)

    def to_heads(a):
        bsz, t_len, _ = a.shape
        return a.reshape(bsz, t_len, MLSTM_HEADS, MLSTM_HEAD_DIM).transpose(0, 2, 1, 3)

    def mlstm_inputs(s):
        q, k, v, g = s[4], s[5], s[6], s[9]
        bsz, t_len, _ = g.shape
        g = (g + gate_b).astype(jnp.float32).reshape(bsz, t_len, 2, 2, MLSTM_HEADS)
        g = jnp.transpose(g, (2, 3, 0, 4, 1))
        return to_heads(q), to_heads(k) * MLSTM_K_SCALE, to_heads(v), g

    qc, kc, vc, gc = mlstm_inputs(s_ctx)
    ql, kl, vl, gl = mlstm_inputs(s_lat)
    h_ctx, h_lat = 0.0, 0.0
    for direction in range(2):
        f = (lambda a: jnp.flip(a, axis=2)) if direction == 1 else (lambda a: a)
        hc, st = mlstm_chunkwise(f(qc), f(kc), f(vc), f(gc[direction, 0]),
                                 jax.nn.log_sigmoid(f(gc[direction, 1])), mlstm_zero_state(qc.shape[0]))
        hl, _ = mlstm_chunkwise(f(ql), f(kl), f(vl), f(gl[direction, 0]),
                                jax.nn.log_sigmoid(f(gl[direction, 1])), st)
        h_lat = h_lat + f(hl)
        if need_ctx:
            h_ctx = h_ctx + f(hc)

    def mlstm_branch(h, s):
        o, z = s[7], s[8]
        bsz, t_len, _ = o.shape
        h = h.transpose(0, 2, 1, 3).reshape(bsz, t_len, MLSTM_DIM).astype(o.dtype)
        return jax.nn.sigmoid(o) * h * jax.nn.silu(z)

    def merge(s, h):
        return jnp.concatenate([conv_branch(s), mlstm_branch(h, s)], axis=-1) @ w_out

    y_lat = merge(s_lat, h_lat)
    y_ctx = merge(s_ctx, h_ctx) if need_ctx else None
    return y_ctx, y_lat

def mla_attend(q_n, q_r, k_n, k_r, v):
    s = jnp.einsum('bqhd,bkhd->bhqk', q_n, k_n) + jnp.einsum('bqhr,bkr->bhqk', q_r, k_r)
    p = jax.nn.softmax(s.astype(jnp.float32) * MLA_SCALE, axis=-1)
    return jnp.einsum('bhqk,bkhd->bqhd', p.astype(v.dtype), v)

def mla_mixer(u_ctx, u_lat, w_in, q_norm, w_uq, kv_norm, w_ukv, w_out, cos, sin, need_ctx):
    s_ctx = split_cols(u_ctx @ w_in, ODD_IN_SIZES)
    s_lat = split_cols(u_lat @ w_in, ODD_IN_SIZES)

    def kv_side(s):
        kv_c, k_r = s[1], s[2]
        bsz, t_len, _ = kv_c.shape
        kv = (rms_norm(kv_c, kv_norm) @ w_ukv).reshape(bsz, t_len, MLA_HEADS, QK_NOPE_DIM + V_HEAD_DIM)
        return kv[..., :QK_NOPE_DIM], k_r, kv[..., QK_NOPE_DIM:]

    def q_side(s):
        q_c = s[0]
        bsz, t_len, _ = q_c.shape
        q = (rms_norm(q_c, q_norm) @ w_uq).reshape(bsz, t_len, MLA_HEADS, QK_NOPE_DIM + QK_ROPE_DIM)
        return q[..., :QK_NOPE_DIM], q[..., QK_NOPE_DIM:]

    kn_c, kr_c, v_c = kv_side(s_ctx)
    kn_l, kr_l, v_l = kv_side(s_lat)
    kr_l = apply_rope(kr_l, cos, sin)
    qn_l, qr_l = q_side(s_lat)
    qr_l = apply_rope(qr_l, cos[:, None, :], sin[:, None, :])
    kn_all = jnp.concatenate([kn_c, kn_l], axis=1)
    kr_all = jnp.concatenate([kr_c, kr_l], axis=1)
    v_all = jnp.concatenate([v_c, v_l], axis=1)
    bsz, n_lat, _ = u_lat.shape
    n_blk = n_lat // Q_BLOCK

    def blocks(a):
        return jnp.moveaxis(a.reshape((bsz, n_blk, Q_BLOCK) + a.shape[2:]), 1, 0)

    o_blk = lax.map(lambda qs: mla_attend(qs[0], qs[1], kn_all, kr_all, v_all), (blocks(qn_l), blocks(qr_l)))
    o_lat = jnp.moveaxis(o_blk, 0, 1).reshape(bsz, n_lat, MLA_DIM)
    y_lat = (o_lat * jax.nn.silu(s_lat[3])) @ w_out
    y_ctx = None
    if need_ctx:
        qn_c, qr_c = q_side(s_ctx)
        o_ctx = mla_attend(qn_c, qr_c, kn_c, kr_c, v_c).reshape(bsz, -1, MLA_DIM)
        y_ctx = (o_ctx * jax.nn.silu(s_ctx[3])) @ w_out
    return y_ctx, y_lat

def setup_inputs(seed: int = 0) -> dict:
    key = jax.random.key(seed)
    ks = jax.random.split(key, 20)

    def nrm(k, shape, s):
        return jax.random.normal(k, shape, jnp.float32) * s

    i_bias = nrm(ks[10], (N_EVEN, 2, 1, MLSTM_HEADS), 0.1)
    f_bias = jnp.linspace(3.0, 6.0, MLSTM_HEADS, dtype=jnp.float32) + nrm(ks[11], (N_EVEN, 2, 1, MLSTM_HEADS), 0.1)
    return {
        'x': nrm(ks[0], (BATCH, SEQ, D_MODEL), 1.0),
        'c': nrm(ks[1], (BATCH, D_MODEL), 1.0),
        'ctx': nrm(ks[2], (BATCH, CTX_LEN, D_MODEL), 1.0),
        'c_ctx': nrm(ks[3], (D_MODEL,), 1.0),
        'mod_w': nrm(ks[4], (DEPTH, D_MODEL, 3 * D_MODEL), 0.5 * D_MODEL ** -0.5),
        'mod_b': nrm(ks[5], (DEPTH, 3 * D_MODEL), 0.01),
        'ln_g': 1.0 + nrm(ks[6], (DEPTH, D_MODEL), 0.01),
        'ln_b': nrm(ks[7], (DEPTH, D_MODEL), 0.01),
        'ev_w_in': nrm(ks[8], (N_EVEN, D_MODEL, EVEN_IN_DIM), D_MODEL ** -0.5),
        'ev_conv_w': nrm(ks[9], (N_EVEN, CONV_WIDTH, CONV_DIM), CONV_WIDTH ** -0.5),
        'ev_gate_b': jnp.concatenate([i_bias, f_bias], axis=2).reshape(N_EVEN, 4 * MLSTM_HEADS),
        'ev_w_out': nrm(ks[12], (N_EVEN, EVEN_MIX_DIM, D_MODEL), DEEPNORM_BETA * EVEN_MIX_DIM ** -0.5),
        'od_w_in': nrm(ks[13], (N_ODD, D_MODEL, ODD_IN_DIM), D_MODEL ** -0.5),
        'od_q_norm': 1.0 + nrm(ks[14], (N_ODD, Q_LORA_RANK), 0.01),
        'od_w_uq': nrm(ks[15], (N_ODD, Q_LORA_RANK, MLA_HEADS * (QK_NOPE_DIM + QK_ROPE_DIM)), Q_LORA_RANK ** -0.5),
        'od_kv_norm': 1.0 + nrm(ks[16], (N_ODD, KV_LORA_RANK), 0.01),
        'od_w_ukv': nrm(ks[17], (N_ODD, KV_LORA_RANK, MLA_HEADS * (QK_NOPE_DIM + V_HEAD_DIM)), KV_LORA_RANK ** -0.5),
        'od_w_out': nrm(ks[18], (N_ODD, MLA_DIM, D_MODEL), DEEPNORM_BETA * MLA_DIM ** -0.5),
    }

def reference(x, c, ctx, c_ctx, mod_w, mod_b, ln_g, ln_b, ev_w_in, ev_conv_w, ev_gate_b, ev_w_out,
              od_w_in, od_q_norm, od_w_uq, od_kv_norm, od_w_ukv, od_w_out):
    cos, sin = axial_rope_tables(x.shape[1])
    silu_c = jax.nn.silu(c)
    silu_cc = jax.nn.silu(c_ctx)
    h_lat, h_ctx = x, ctx
    for layer in range(DEPTH):
        need_ctx = layer < DEPTH - 1
        sh_l, sc_l, g_l = jnp.split((silu_c @ mod_w[layer] + mod_b[layer])[:, None, :], 3, axis=-1)
        sh_c, sc_c, g_c = jnp.split(silu_cc @ mod_w[layer] + mod_b[layer], 3, axis=-1)
        u_lat = h_lat * (1.0 + sc_l) + sh_l
        u_ctx = h_ctx * (1.0 + sc_c) + sh_c
        j = layer // 2
        if layer % 2 == 0:
            y_ctx, y_lat = even_mixer(u_ctx, u_lat, ev_w_in[j], ev_conv_w[j], ev_gate_b[j], ev_w_out[j], need_ctx)
        else:
            y_ctx, y_lat = mla_mixer(u_ctx, u_lat, od_w_in[j], od_q_norm[j], od_w_uq[j], od_kv_norm[j],
                                     od_w_ukv[j], od_w_out[j], cos, sin, need_ctx)
        h_lat = layer_norm(DEEPNORM_ALPHA * h_lat + g_l * y_lat, ln_g[layer], ln_b[layer])
        if need_ctx:
            h_ctx = layer_norm(DEEPNORM_ALPHA * h_ctx + g_c * y_ctx, ln_g[layer], ln_b[layer])
    return h_lat


_drawn_inputs = setup_inputs


def setup_inputs(seed=0):
    import zlib

    import numpy as np

    out = dict(_drawn_inputs(seed))
    spreads = {}
    factors = {'ln_g': 4.055,
     'ln_b': 4.193,
     'od_w_in': 2.99,
     'od_q_norm': 8.0,
     'od_w_uq': 8.0,
     'od_kv_norm': 8.0,
     'od_w_ukv': 2.959,
     'od_w_out': 3.004}
    for name, (base, spread) in spreads.items():
        noise = np.random.default_rng([zlib.crc32(name.encode()), seed]).standard_normal(out[name].shape)
        drawn = base * np.exp(spread * noise) if base else spread * noise
        out[name] = __import__('jax').numpy.asarray(drawn.astype(out[name].dtype))
    for name, factor in factors.items():
        out[name] = (out[name] * factor).astype(out[name].dtype)
    return out
```

```python
import concourse.bass as bass
from concourse import mybir
from contextlib import ExitStack
import numpy as np

D = 1024
CTX, LAT = 256, 1024
T = CTX + LAT
P = 128
KD = D // P
NT = T // P
NC = CTX // P
HEADS, HD = 4, 256
MIX = 2048
KM = MIX // P
AH, DN, DR = 16, 128, 64
QR, KVR = 384, 256
CHUNKS = [(0, 256), (256, 512), (768, 512)]
NEG = -1e30
ALPHA = float(4 ** 0.25)
LN_EPS, RMS_EPS = 1e-5, 1e-6
ATT_SCALE = float((DN + DR) ** -0.5)
K_SCALE = float(HD ** -0.5)

F32, F32R, BF16 = mybir.dt.float32, mybir.dt.float32r, mybir.dt.bfloat16
ACT = mybir.ActivationFunctionType
ALU = mybir.AluOpType
AX = mybir.AxisListType.X


def f(ap):
    return ap.bitcast(F32)


def mm3(nc, out, w, x, first=True, last=True):
    (whi, wlo), (xhi, xlo) = w, x
    nc.tensor.matmul(out, whi, xhi, start=first, stop=False)
    nc.tensor.matmul(out, whi, xlo, start=False, stop=False)
    return nc.tensor.matmul(out, wlo, xhi, start=False, stop=last)


class Space:

    def __init__(self, nc, ctx, tag):
        self.nc, self.tag = nc, tag
        self.ctx, self.sems = ctx, []
        ctx.callback(self.close)

    def close(self):
        if self.sems:
            self.nc.clear_and_free_semaphores(self.sems)
            self.nc.all_engine_barrier()

    def sb(self, name, shape, dt=F32):
        return self.ctx.enter_context(self.nc.sbuf_tensor(f"{self.tag}_{name}", shape, dt))

    def bank(self, name, banks=1):
        return self.ctx.enter_context(self.nc.psum_tensor(f"{self.tag}_{name}", [P, 512 * banks], F32))

    def sem(self, name):
        self.sems.append(self.nc.alloc_semaphore(name=f"{self.tag}_{name}"))
        return self.sems[-1]

    def pair(self, name, shape):
        return self.sb(name + "_hi", shape, F32R), self.sb(name + "_lo", shape, F32R)


def stage_modulate(nc, a, keep):
    NCH, CW = 12, 256
    u_hi, u_lo, mod_col, ident = keep["u_hi"], keep["u_lo"], keep["mod_col"], keep["ident"]
    with ExitStack() as ctx:
        s = Space(nc, ctx, "m")
        xT = s.sb("xT", [P, KD, T])
        x_tok = [s.sb(f"x_tok{i}", [P, D]) for i in range(2)]
        w_raw = [s.sb(f"w_raw{i}", [P, KD, CW]) for i in range(2)]
        w = [s.pair(f"w{i}", [P, KD, CW]) for i in range(2)]
        sel = s.sb("sel", [5, 2])
        rows = s.sb("rows", [5, 3 * D])
        g_row = s.sb("g_row", [2, 2, D])
        c_row, c_tanh = s.sb("c_row", [2 * KD, P]), s.sb("c_tanh", [2 * KD, P])
        c_silu = s.sb("c_silu", [P, 2 * KD])
        cs = s.sb("cs", [P, KD, P], F32R)
        tp_bank = [s.bank(f"tp{i}") for i in range(4)]
        mod_bank = [s.bank(f"mod{i}") for i in range(2)]
        col_bank, row_bank = s.bank("col"), s.bank("row")
        x_in = [s.sem(f"x_in{i}") for i in range(2)]
        w_in = [s.sem(f"w_in{i}") for i in range(2)]
        c_in, const_in, bias_in = s.sem("c_in"), s.sem("const_in"), s.sem("bias_in")
        tp, tp_free = s.sem("tp"), s.sem("tp_free")
        c_t, c_s, cs_hi, cs_zero, cs_lo = s.sem("c_t"), s.sem("c_s"), s.sem("cs_hi"), s.sem("cs_zero"), s.sem("cs_lo")
        w_hi, w_split = s.sem("w_hi"), s.sem("w_split")
        mod_done, mod_free = s.sem("mod_done"), s.sem("mod_free")
        cols_done, cols_kept, plus_one = s.sem("cols_done"), s.sem("cols_kept"), s.sem("plus_one")
        grow_done, grow_kept, grow_out = s.sem("grow_done"), s.sem("grow_kept"), s.sem("grow_out")
        u_f32, u_hi_done, u_lo_done = s.sem("u_f32"), s.sem("u_hi_done"), s.sem("u_lo_done")
        w_src = a["mod_w"].rearrange("l (k p) n -> l p k n", p=P)
        h0_src = a["h0"].rearrange("(n p) d -> p n d", p=P)
        block = ctx.enter_context(nc.Block())

        @block.sync
        def _(sp):
            sp.dma_start(ident[:, :], a["c_ident"]).then_inc(const_in, 16)
            sp.dma_start(sel[:, :], a["c_sel"]).then_inc(const_in, 16)
            sp.dma_start(c_row[0:KD, :], a["c"].rearrange("a (k p) -> (a k) p", p=P)).then_inc(c_in, 16)
            sp.dma_start(c_row[KD:2 * KD, :], a["c_ctx"].rearrange("(k p) -> k p", p=P)).then_inc(c_in, 16)
            for l in range(2):
                if l == 1:
                    sp.wait_ge(grow_done, 2)
                sp.dma_start(rows[4:5, :], a["mod_b"][l:l + 1, :]).then_inc(bias_in, 16)
                with sp.Fori(0, NCH // 2) as i:
                    for b in range(2):
                        sp.wait_ge(w_split, i * 2 + (NCH * l + b + 1))
                        sp.dma_start(w_raw[b][:, :, :], w_src[l][:, :, bass.ds(i * (2 * CW) + b * CW, CW)]).then_inc(w_in[b], 16)
            sp.wait_ge(grow_kept, 4)
            sp.dma_start(a["g_rows"].rearrange("l v d -> v l d"), g_row[:, :, :]).then_inc(grow_out, 16)
            sp.wait_ge(grow_out, 16)

        @block.scalar
        def _(act):
            act.wait_ge(c_in, 32)
            nc.scalar.activation(c_tanh[:, :], c_row[:, :], ACT.Tanh, scale=0.5).then_inc(c_t, 1)
            act.wait_ge(c_s, 3)
            act.wait_ge(cs_zero, 1)
            nc.scalar.copy(cs[:, :, 0:2], c_silu[:, :].rearrange("p (v k) -> p k v", v=2)).then_inc(cs_hi, 1)
            for l in range(2):
                if l == 1:
                    act.wait_ge(grow_done, 2)
                with act.Fori(0, NCH // 2) as i:
                    for b in range(2):
                        act.wait_ge(w_in[b], i * 16 + (16 * (NCH // 2) * l + 16))
                        act.wait_ge(mod_done, i * 2 + (NCH * l + b + 1))
                        nc.scalar.copy(w[b][0][:, :, :], w_raw[b][:, :, :]).then_inc(w_hi, 1)
                    for b in range(2):
                        act.wait_ge(mod_done, i * 2 + (NCH * l + b + 3))
                        nc.scalar.copy(rows[0:4, bass.ds(i * (2 * CW) + b * CW, CW)], mod_bank[b][0:4, 0:CW]).then_inc(mod_free, 1)
                act.wait_ge(cols_done, l + 1)
                nc.scalar.copy(mod_col[:, l, :, :], col_bank[:, 0:48].rearrange("p (j v) -> p j v", v=2)).then_inc(cols_kept, 1)
                for j in range(2):
                    act.wait_ge(grow_done, 2 * l + j + 1)
                    nc.scalar.copy(g_row[:, l, 512 * j:512 * j + 512], row_bank[0:2, :]).then_inc(grow_kept, 1)
            for k in range(KD):
                act.wait_ge(u_f32, 2 * k + 2)
                nc.scalar.copy(u_hi[:, k, :], xT[:, k, :]).then_inc(u_hi_done, 1)

        @block.vector
        def _(dve):
            dve.sem_inc(tp_free, 4)
            dve.sem_inc(w_split, 2)
            nc.vector.memset(f(cs[:, :, :]), 0.0).then_inc(cs_zero, 1)
            dve.wait_ge(c_t, 1)
            nc.vector.scalar_tensor_tensor(c_tanh[:, :], c_tanh[:, :], 1.0, c_row[:, :], ALU.add, ALU.mult).then_inc(c_s, 1)
            dve.wait_ge(c_s, 2)
            nc.vector.tensor_scalar(c_silu[:, :], col_bank[:, 0:2 * KD], 0.5, None, ALU.mult).then_inc(c_s, 1)
            dve.wait_ge(cs_hi, 1)
            nc.vector.tensor_tensor(cs[:, :, 2:4], c_silu[:, :].rearrange("p (v k) -> p k v", v=2), f(cs[:, :, 0:2]), ALU.subtract).then_inc(cs_lo, 1)
            with dve.Fori(0, NT // 2) as i:
                for b in range(2):
                    for g in range(2):
                        dve.wait_ge(tp, i * 4 + (2 * b + g + 1))
                        nc.vector.tensor_copy(xT[:, 4 * g:4 * g + 4, bass.ds(i * 256 + b * P, P)],
                                              tp_bank[2 * b + g][:, :].rearrange("p (k t) -> p k t", t=P)).then_inc(tp_free, 1)
            for l in range(2):
                with dve.Fori(0, NCH // 2) as i:
                    for b in range(2):
                        dve.wait_ge(w_hi, i * 2 + (NCH * l + b + 1))
                        nc.vector.tensor_tensor(w[b][1][:, :, :], w_raw[b][:, :, :], f(w[b][0][:, :, :]), ALU.subtract).then_inc(w_split, 1)
                dve.wait_ge(cols_kept, l + 1)
                nc.vector.tensor_scalar(mod_col[:, l, KD:2 * KD, :], mod_col[:, l, KD:2 * KD, :], 1.0, None, ALU.add).then_inc(plus_one, 1)
            dve.wait_ge(plus_one, 2)
            dve.wait_ge(tp_free, 4 + 2 * NT)
            for k in range(KD + 1):
                if k < KD:
                    for v, t0, n in ((1, 0, CTX), (0, CTX, LAT)):
                        nc.vector.tensor_scalar(xT[:, k, t0:t0 + n], xT[:, k, t0:t0 + n], mod_col[:, 0, KD + k, v:v + 1],
                                                mod_col[:, 0, k, v:v + 1], ALU.mult, ALU.add).then_inc(u_f32, 1)
                if k:
                    dve.wait_ge(u_hi_done, k)
                    nc.vector.tensor_tensor(u_lo[:, k - 1, :], xT[:, k - 1, :], f(u_hi[:, k - 1, :]), ALU.subtract).then_inc(u_lo_done, 1)

        @block.gpsimd
        def _(pool):
            pool.sem_inc(mod_done, 2)
            pool.sem_inc(mod_free, 2)
            with pool.Fori(0, NT // 2) as i:
                for b in range(2):
                    pool.wait_ge(tp_free, i * 4 + (2 * b + 2))
                    pool.dma_start(x_tok[b][:, :], h0_src[:, bass.ds(i * 2 + b, 1), :]).then_inc(x_in[b], 16)

        @block.tensor
        def _(pe):
            pe.wait_ge(const_in, 32)
            pe.wait_ge(c_s, 1)
            nc.tensor.transpose(col_bank[:, 0:2 * KD], c_tanh[:, :], ident[0:2 * KD, 0:2 * KD]).then_inc(c_s, 1)
            with pe.Fori(0, NT // 2) as i:
                for b in range(2):
                    pe.wait_ge(x_in[b], i * 16 + 16)
                    for g in range(2):
                        pe.wait_ge(tp_free, i * 4 + (2 * b + g + 1))
                        for k in range(4):
                            last = nc.tensor.transpose(tp_bank[2 * b + g][:, k * P:(k + 1) * P],
                                                       x_tok[b][:, (4 * g + k) * P:(4 * g + k + 1) * P], ident[:, :])
                        last.then_inc(tp, 1)
            pe.wait_ge(cs_lo, 1)
            for l in range(2):
                with pe.Fori(0, NCH // 2) as i:
                    for b in range(2):
                        pe.wait_ge(w_split, i * 2 + (NCH * l + b + 3))
                        pe.wait_ge(mod_free, i * 2 + (NCH * l + b + 1))
                        for k in range(KD):
                            nc.tensor.matmul(mod_bank[b][:, 0:CW], cs[:, k, :], w[b][0][:, k, :], start=k == 0, stop=False)
                            last = nc.tensor.matmul(mod_bank[b][:, 0:CW], cs[:, k, :], w[b][1][:, k, :], start=False, stop=k == KD - 1)
                        last.then_inc(mod_done, 1)
                pe.wait_ge(mod_free, 2 + NCH * (l + 1))
                pe.wait_ge(bias_in, 16 * (l + 1))
                if l:
                    pe.wait_ge(cols_kept, l)
                for j in range(24):
                    last = nc.tensor.matmul(col_bank[:, 2 * j:2 * j + 2], rows[0:5, j * P:(j + 1) * P], sel[0:5, :], start=True, stop=True)
                last.then_inc(cols_done, 1)
                for j in range(2):
                    if 2 * l + j:
                        pe.wait_ge(grow_kept, 2 * l + j)
                    nc.tensor.matmul(row_bank[0:2, :], sel[0:5, :], rows[0:5, 2 * D + 512 * j:2 * D + 512 * j + 512],
                                     start=True, stop=True).then_inc(grow_done, 1)


def stage_gates(nc, a, keep):
    R36 = 36
    u_hi, u_lo, ident, gate_col = keep["u_hi"], keep["u_lo"], keep["ident"], keep["gate_col"]
    with ExitStack() as ctx:
        s = Space(nc, ctx, "g")
        w_raw = s.sb("w_raw", [P, KD, 16])
        w_hi, w_lo = s.pair("w", [P, KD, P])
        bias = s.sb("bias", [P, 1])
        row = {n: s.sb(n, [R36, NT, P]) for n in ("i", "f", "e", "b", "m", "keep", "R", "ai", "wt", "em", "dec")}
        mst, dm, mnew, bsum, dec_c = (s.sb(n, [R36, NT]) for n in ("mst", "dm", "mnew", "bsum", "dec_c"))
        gate_bank = [s.bank(f"gate{i}") for i in range(3)]
        col_bank = [s.bank(f"col{i}") for i in range(5)] + gate_bank[:1]
        w_in, bias_in, zeroed = s.sem("w_in"), s.sem("bias_in"), s.sem("zeroed")
        hi_done, lo_done, gate_done = s.sem("hi_done"), s.sem("lo_done"), s.sem("gate_done")
        i_row, f_row, f_log, logf = (s.sem(n) for n in ("i_row", "f_row", "f_log", "logf"))
        act_step, dve_step, cols_done, cols_kept = (s.sem(n) for n in ("act_step", "dve_step", "cols_done", "cols_kept"))
        rows2 = lambda name: row[name][:, :, :].rearrange("r c t -> r (c t)")
        order = ["G", "R", "ai", "wt", "em", "dec"]
        row["G"] = row["i"]
        G0 = 4 * D + 5 * D
        block = ctx.enter_context(nc.Block())

        @block.sync
        def _(sp):
            sp.dma_start(w_raw[:, :, :], a["ev_w_in"].rearrange("a (k p) n -> p (a k) n", p=P)[:, :, G0:G0 + 16]).then_inc(w_in, 16)
            sp.wait_ge(zeroed, 1)
            for d in range(2):
                for g in range(2):
                    c = 8 * d + 4 * g
                    sp.dma_start(bias[64 * g + 32 * d:64 * g + 32 * d + 4, :],
                                 a["ev_gate_b"].rearrange("a n -> n a")[c:c + 4, :]).then_inc(bias_in, 16)

        def split_cols(tile, d, g):
            return tile[:, :, 64 * g + 32 * d:64 * g + 32 * d + 4]

        def raw_cols(d, g):
            return w_raw[:, :, 8 * d + 4 * g:8 * d + 4 * g + 4]

        @block.scalar
        def _(act):
            act.wait_ge(w_in, 16)
            act.wait_ge(zeroed, 3)
            for d in range(2):
                for g in range(2):
                    nc.scalar.copy(split_cols(w_hi, d, g), raw_cols(d, g)).then_inc(hi_done, 1)
            act.wait_ge(bias_in, 64)
            for j, (t0, n) in enumerate(CHUNKS):
                act.wait_ge(gate_done, j + 1)
                nc.scalar.activation(rows2("i")[:, t0:t0 + n], gate_bank[j][0:R36, 0:n], ACT.Identity,
                                     bias=bias[0:R36, :]).then_inc(i_row, 1)
                nc.scalar.activation(rows2("f")[:, t0:t0 + n], gate_bank[j][64:64 + R36, 0:n], ACT.Identity,
                                     bias=bias[64:64 + R36, :]).then_inc(f_row, 1)
            act.wait_ge(f_row, 3)
            nc.scalar.activation(rows2("e"), rows2("f"), ACT.Abs).then_inc(act_step, 1)
            act.wait_ge(act_step, 1)
            nc.scalar.activation(rows2("e"), rows2("e"), ACT.Exp, scale=-1.0).then_inc(act_step, 1)
            act.wait_ge(act_step, 2)
            nc.scalar.activation(rows2("e"), rows2("e"), ACT.Ln, bias=1.0).then_inc(f_log, 1)
            act.wait_ge(logf, 9)
            for n in ("ai", "wt"):
                nc.scalar.activation(rows2(n), rows2(n), ACT.Exp).then_inc(act_step, 1)
            nc.scalar.activation(rows2("em"), rows2("m"), ACT.Exp, scale=-1.0).then_inc(act_step, 1)
            nc.scalar.activation(dec_c[:, :], mst[:, :], ACT.Exp).then_inc(act_step, 1)

        @block.vector
        def _(dve):
            nc.vector.memset(bias[:, :], 0.0).then_inc(zeroed, 1)
            nc.vector.memset(f(w_hi[:, :, :]), 0.0).then_inc(zeroed, 1)
            nc.vector.memset(f(w_lo[:, :, :]), 0.0).then_inc(zeroed, 1)
            dve.wait_ge(zeroed, 3)
            for d in range(2):
                for g in range(2):
                    dve.wait_ge(hi_done, 2 * d + g + 1)
                    nc.vector.tensor_tensor(split_cols(w_lo, d, g), raw_cols(d, g), f(split_cols(w_hi, d, g)), ALU.subtract).then_inc(lo_done, 1)
            nc.vector.memset(rows2("b"), 0.0)
            nc.vector.memset(rows2("m"), 0.0)
            nc.vector.memset(rows2("keep"), 1.0)
            nc.vector.memset(mst[:, :], NEG)
            nc.vector.memset(mnew[:, :], 0.0)
            nc.vector.memset(bsum[:, :], 0.0).then_inc(dve_step, 1)
            dve.wait_ge(dve_step, 1)
            nc.vector.memset(row["keep"][0:4, :, 0], 0.0)
            nc.vector.memset(row["keep"][32:36, :, P - 1], 0.0).then_inc(dve_step, 1)
            dve.wait_ge(f_row, 3)
            dve.wait_ge(f_log, 1)
            dve.wait_ge(i_row, 3)
            nc.vector.scalar_tensor_tensor(rows2("f"), rows2("f"), 0.0, rows2("e"), ALU.min, ALU.subtract).then_inc(logf, 1)
            dve.wait_ge(logf, 1)
            dve.wait_ge(dve_step, 2)
            F_, B_ = slice(0, 4), slice(32, 36)
            b2, m2, f2, i2, k2 = rows2("b"), rows2("m"), rows2("f"), rows2("i"), rows2("keep")
            scan = nc.vector.tensor_tensor_scan
            scan(b2[F_], k2[F_], f2[F_], 0.0, ALU.mult, ALU.add)
            scan(b2[B_, ::-1], k2[B_, ::-1], f2[B_, ::-1], 0.0, ALU.mult, ALU.add).then_inc(logf, 1)
            scan(m2[F_], f2[F_], i2[F_], NEG, ALU.add, ALU.max)
            scan(m2[B_, CTX - 1::-1], f2[B_, CTX - 1::-1], i2[B_, CTX - 1::-1], NEG, ALU.add, ALU.max).then_inc(logf, 1)
            dve.wait_ge(logf, 3)
            scan(m2[B_, :CTX - 1:-1], f2[B_, :CTX - 1:-1], i2[B_, :CTX - 1:-1], m2[B_, 0:1], ALU.add, ALU.max).then_inc(logf, 1)
            dve.wait_ge(logf, 4)
            m, b = row["m"], row["b"]
            nc.vector.tensor_copy(mst[F_, 1:NT], m[F_, 0:NT - 1, P - 1])
            nc.vector.tensor_copy(mst[B_, 0:1], m[B_, 1, 0:1])
            nc.vector.tensor_copy(mst[B_, 2:NT - 1], m[B_, 3:NT, 0])
            nc.vector.tensor_copy(mst[B_, NT - 1:NT], m[B_, 0, 0:1])
            nc.vector.tensor_copy(mnew[F_, :], m[F_, :, P - 1])
            nc.vector.tensor_copy(mnew[B_, :], m[B_, :, 0])
            nc.vector.tensor_copy(bsum[F_, :], b[F_, :, P - 1])
            nc.vector.tensor_copy(bsum[B_, :], b[B_, :, 0]).then_inc(logf, 1)
            dve.wait_ge(logf, 5)
            nc.vector.tensor_tensor(dm[:, :], bsum[:, :], mnew[:, :], ALU.subtract)
            nc.vector.tensor_tensor(rows2("R"), b2, m2, ALU.subtract)
            nc.vector.tensor_tensor(rows2("G"), i2, b2, ALU.subtract).then_inc(logf, 1)
            dve.wait_ge(logf, 6)
            spread = lambda t: t[:, :].unsqueeze(2).broadcast_to([R36, NT, P])
            nc.vector.tensor_tensor(row["ai"][:, :, :], row["R"][:, :, :], spread(mst), ALU.add).then_inc(logf, 1)
            nc.vector.tensor_tensor(row["wt"][:, :, :], row["G"][:, :, :], spread(dm), ALU.add).then_inc(logf, 1)
            dve.wait_ge(logf, 8)
            nc.vector.tensor_tensor(mst[:, :], mst[:, :], dm[:, :], ALU.add).then_inc(logf, 1)
            dve.wait_ge(act_step, 6)
            nc.vector.tensor_copy(row["dec"][:, :, :], spread(dec_c)).then_inc(dve_step, 1)
            for q in range(6):
                dve.wait_ge(cols_done, q + 1)
                bank = col_bank[q][:, 0:NT * R36].rearrange("p (c r) -> p c r", r=R36)
                for d in range(2):
                    nc.vector.tensor_copy(gate_col[:, q, :, 4 * d:4 * d + 4], bank[:, :, 32 * d:32 * d + 4]).then_inc(cols_kept, 1)

        @block.tensor
        def _(pe):
            pe.wait_ge(lo_done, 4)
            for j, (t0, n) in enumerate(CHUNKS):
                for k in range(KD):
                    last = mm3(nc, gate_bank[j][:, 0:n], (w_hi[:, k, :], w_lo[:, k, :]),
                               (u_hi[:, k, t0:t0 + n], u_lo[:, k, t0:t0 + n]), k == 0, k == KD - 1)
                last.then_inc(gate_done, 1)
            pe.wait_ge(dve_step, 3)
            for q, name in enumerate(order):
                for c in range(NT):
                    last = nc.tensor.transpose(col_bank[q][:, c * R36:(c + 1) * R36], row[name][:, c, :], ident[0:R36, 0:R36])
                last.then_inc(cols_done, 1)


def stage_even(nc, a, keep):
    u_hi, u_lo, ident, gate_col = keep["u_hi"], keep["u_lo"], keep["ident"], keep["gate_col"]
    TILES = [(4 * D, HD), (4 * D + P, HD), (5 * D, HD), (5 * D + P, HD), (6 * D, HD), (6 * D + P, HD)]
    KIND = ["q", "q", "k", "k", "v", "v"]
    for j in range(2):
        TILES += [(D + P * j, HD), (2 * D + P * j, HD), (P * j, HD), (3 * D + P * j, HD)]
        KIND += ["conv_c", "conv_x", "conv_b", "conv_z"]
    for j in range(2):
        TILES += [(7 * D + P * j, HD), (8 * D + P * j, HD)]
        KIND += ["out_o", "out_z"]
    NTILE = len(TILES)
    NSTEP = 2 * NT
    BWD = [1, 0] + list(range(NT - 1, 1, -1))
    FIRST_STEP_TILE = 7
    BY_ACT = ("v", "conv_c", "out_o")
    A_TILES = [t for t in range(NTILE) if KIND[t] in BY_ACT]
    D_TILES = [t for t in range(NTILE) if KIND[t] not in BY_ACT]

    with ExitStack() as ctx:
        s = Space(nc, ctx, "v")
        w_raw = s.sb("w_raw", [P, KD, P])
        w = [s.pair(f"w{i}", [P, KD, P]) for i in range(2)]
        q_hi, q_lo = s.pair("q", [P, 2, T])
        k_hi, k_lo = s.pair("kk", [P, 2, T])
        v_hi, v_lo = s.pair("vv", [P, NT, HD + 2])
        h_tok = s.sb("h_tok", [P, NT, HD])
        c_f32 = [s.sb(f"c_f32{d}", [P, 2, HD + 2]) for d in range(2)]
        c_st = [s.pair(f"c_st{d}", [P, 2, HD + 2]) for d in range(2)]
        kw = [s.pair(f"kw{d}", [P, HD]) for d in range(2)]
        wgt = [s.sb(f"wgt{d}", [P, P]) for d in range(2)]
        diag = [s.sb(f"diag{d}", [P, P]) for d in range(2)]
        sw = [s.pair(f"sw{d}", [P, P]) for d in range(2)]
        num = [s.sb(f"num{d}", [P, HD + 2]) for d in range(2)]
        den = [s.sb(f"den{d}", [P, 1]) for d in range(2)]
        rec = [s.sb(f"rec{d}", [P, 1]) for d in range(2)]
        hc = s.sb("hc", [P, 6, NT, 2])
        mask = s.sb("mask", [P, 2, P], BF16)
        ident_b = s.sb("ident_b", [P, P], BF16)
        ident_r = s.sb("ident_r", [P, P], F32R)
        ones = s.sb("ones", [P, P])
        ones_r = s.sb("ones_r", [P, 2], F32R)
        conv_w = s.sb("conv_w", [P, 2, 3])
        buf = [s.sb(f"buf{i}", [P, T + 4]) for i in range(2)]

        pj = [s.bank(f"pj{j}") for j in range(3)]
        sek = [s.bank(f"sek{d}") for d in range(2)]
        x_bank, y_bank, z_bank = s.bank("x"), s.bank("y"), s.bank("z")
        X, Y = x_bank[:, 0:HD + 2], y_bank[:, 0:HD + 2]
        Y_n = y_bank[:, HD + 2:HD + 6].rearrange("p (j c) -> p j c", c=2)
        Z = z_bank[:, :].rearrange("p (j c) -> p j c", c=HD)

        raw_in, seen, bufs_free = s.sem("raw_in"), s.sem("seen"), s.sem("bufs_free")
        const_in, const_ok, cw_in, cw_used = s.sem("const_in"), s.sem("const_ok"), s.sem("cw_in"), s.sem("cw_used")
        w_hi_ok, w_ok = s.sem("w_hi_ok"), s.sem("w_ok")
        pj_done, pj_free_a, pj_free_d = s.sem("pj_done"), s.sem("pj_free_a"), s.sem("pj_free_d")
        half = s.sem("half")
        vt, vt_hi, vt_ok = s.sem("vt"), s.sem("vt_hi"), s.sem("vt_ok")
        conv_tap, conv_mid, gate_part, mix_ready, mix_out = (s.sem(n) for n in ("conv_tap", "conv_mid", "gate_part", "mix_ready", "mix_out"))
        hc_ok, diag_ok, sc_done, wgt_ok, kw_hi_ok, sw_f_ok, sw_hi_ok, kw_lo_ok, sw_ok = (s.sem(n) for n in (
            "hc_ok", "diag_ok", "sc_done", "wgt_ok", "kw_hi_ok", "sw_f_ok", "sw_hi_ok", "kw_lo_ok", "sw_ok"))
        st_done, inter_ok, num_ok, den_ok, rec_ok, h_ok, c_f_ok, c_hi_ok, step_ok = (s.sem(n) for n in (
            "st_done", "inter_ok", "num_ok", "den_ok", "rec_ok", "h_ok", "c_f_ok", "c_hi_ok", "step_ok"))
        ht, ht_used = s.sem("ht"), s.sem("ht_used")
        w_src = a["ev_w_in"].rearrange("a (k p) n -> p (a k) n", p=P)
        mix_rows = a["mixT"].rearrange("(j p) t -> j p t", p=P)
        block = ctx.enter_context(nc.Block())

        def span(b, j):
            t0, n = CHUNKS[j]
            t0 += 1 if j == 0 else 3
            return b[:, t0:t0 + n]

        def tan(t, j):
            if t in (9, 13):
                return span(buf[0], j)
            return span(buf[1], j) if t == 15 else c_f32[0][:, :, :].rearrange("p a b -> p (a b)")[:, 0:CHUNKS[j][1]]

        def load_w(sp, i, t):
            base, stride = TILES[t % NTILE]
            first = base + stride * (t // NTILE)
            sp.wait_ge(w_ok, i * NTILE + t)
            if first == 0:
                sp.sem_inc(seen, 1)
            sp.dma_start(w_raw[:, :, :], w_src[:, :, bass.ds(i * stride + first, P)]).then_inc(raw_in, 16)

        def conv_pass(c):
            return (c - 6) // 4

        @block.sync
        def _(sp):
            sp.dma_start(buf[0][:, 0:2 * P].rearrange("p (d t) -> p d t", d=2), a["c_mask"].rearrange("d s t -> s d t")).then_inc(const_in, 16)
            sp.dma_start(w_raw[:, :, :], w_src[:, :, TILES[0][0]:TILES[0][0] + P]).then_inc(raw_in, 16)

            def store(i, which, row0, done):
                rows = mix_rows[bass.ds(i * 2 + row0, 1)]
                sp.dma_start(rows[:, :, 0:CTX], buf[which][:, 1:1 + CTX]).then_inc(mix_out, 16)
                sp.dma_start(rows[:, :, CTX:T], buf[which][:, CTX + 3:T + 3]).then_inc(mix_out, 16)

            sp.sem_inc(bufs_free, 1)
            with sp.Fori(0, HEADS) as i:
                stored = sp.snap(i * 4)
                sp.wait_ge(cw_used, i * 6 + 1)
                sp.dma_start(conv_w[:, :, :], a["conv_t"].rearrange("(n j p) w -> n p j w", p=P, j=2)[bass.ds(i, 1)].rearrange("n p j w -> p (n j) w")).then_inc(cw_in, 16)
                for t in range(NTILE):
                    load_w(sp, i, t + 1)
                    if t == 10:
                        sp.wait_ge(mix_ready, stored + 1)
                        store(i, 1, 0, None)
                    if t == 14:
                        sp.wait_ge(mix_ready, stored + 2)
                        store(i, 1, 1, None)
                for j in range(2):
                    sp.wait_ge(mix_ready, stored + (3 + j))
                    store(i, j, KD + j, None)
                sp.wait_ge(mix_out, i * 128 + 128)
                sp.sem_inc(bufs_free, 1)
            sp.wait_ge(mix_out, 16 * 8 * HEADS)

        @block.scalar
        def _(act):
            act.wait_ge(const_in, 16)
            nc.scalar.copy(mask[:, :, :], buf[0][:, 0:2 * P].rearrange("p (d t) -> p d t", d=2))
            nc.scalar.copy(ident_b[:, :], ident[:, :])
            nc.scalar.copy(ident_r[:, :], ident[:, :]).then_inc(const_ok, 1)

            def split(i, t, wait_slot=True):
                b = t % 2
                act.wait_ge(raw_in, i * (16 * NTILE) + 16 * (t + 1))
                if wait_slot:
                    act.wait_ge(pj_done, i * (3 * NTILE) + 3 * (t - 1))
                nc.scalar.copy(w[b][0][:, :, :], w_raw[:, :, :]).then_inc(w_hi_ok, 1)

            def evacuate(i, t, j):
                kind, (t0, n) = KIND[t], CHUNKS[j]
                act.wait_ge(pj_done, i * (3 * NTILE) + 3 * t + j + 1)
                src = pj[j][:, 0:n]
                if kind == "q":
                    nc.scalar.copy(q_hi[:, t, t0:t0 + n], src).then_inc(half, 1)
                elif kind == "k":
                    nc.scalar.mul(k_hi[:, t - 2, t0:t0 + n], src, K_SCALE).then_inc(half, 1)
                elif kind == "v":
                    act.wait_ge(bufs_free, i + 1)
                    nc.scalar.copy(span(buf[t - 4], j), src).then_inc(pj_free_a, 1)
                elif kind == "conv_c":
                    if t == 6:
                        act.wait_ge(vt, i * 6 + 3)
                    else:
                        act.wait_ge(gate_part, i * 12 + 4)
                    nc.scalar.copy(span(buf[0], j), src).then_inc(pj_free_a, 1)
                elif kind == "conv_z" or kind == "out_z":
                    act.wait_ge(gate_part, i * 12 + {9: 0, 13: 3, 15: 6, 17: 9}[t] + j + 1)
                    if t == 9 or t == 13:
                        act.wait_ge(conv_tap, i * 6 + (3 if t == 9 else 6))
                    if t == 15:
                        act.wait_ge(mix_out, i * 128 + 64)
                    nc.scalar.activation(tan(t, j), src, ACT.Tanh, scale=0.5).then_inc(half, 1)
                elif kind == "out_o":
                    which = (t - 14) // 2
                    act.wait_ge(gate_part, i * 12 + 6 + 3 * which + 1)
                    nc.scalar.activation(span(buf[which], j), src, ACT.Tanh, scale=0.5).then_inc(pj_free_a, 1)

            def tap1(i, t):
                j = conv_pass(t)
                act.wait_ge(cw_in, i * 16 + 16)
                act.wait_ge(conv_tap, i * 6 + 3 * j + 1)
                if j == 0:
                    act.wait_ge(vt, i * 6 + 6)
                else:
                    act.wait_ge(mix_out, i * 128 + 32)
                nc.scalar.mul(buf[1][:, 1:T + 3], buf[0][:, 1:T + 3], conv_w[:, j, 1:2]).then_inc(conv_mid, 1)

            def v_hi_part(i, j, g):
                c0, nch = ((0, 2), (2, 4), (6, 4))[g]
                act.wait_ge(vt, i * 6 + 3 * j + g + 1)
                src = (x_bank, y_bank, z_bank)[g][:, 0:nch * P].rearrange("p (c e) -> p c e", e=P)
                nc.scalar.copy(v_hi[:, c0:c0 + nch, j * P:(j + 1) * P], src).then_inc(vt_hi, 1)

            def weights(i, n, d):
                c, g = (n if d == 0 else BWD[n]), 2 * n + d
                if n == 0:
                    act.wait_ge(hc_ok, i + 1)
                act.wait_ge(sc_done, i * NSTEP + g + 1)
                nc.scalar.activation(wgt[d][:, :], sek[d][:, P:2 * P], ACT.Exp, bias=hc[:, 0, c, d:d + 1]).then_inc(wgt_ok, 1)
                nc.scalar.mul(kw[d][0][:, :], sek[d][:, 2 * P:4 * P], hc[:, 3, c, d:d + 1]).then_inc(kw_hi_ok, 1)

            def scores_hi(i, n, d):
                act.wait_ge(sw_f_ok, i * NSTEP + 2 * n + d + 1)
                nc.scalar.copy(sw[d][0][:, :], wgt[d][:, :]).then_inc(sw_hi_ok, 1)

            def after_state(i, n, d):
                c, g = (n if d == 0 else BWD[n]), 2 * n + d
                act.wait_ge(st_done, i * NSTEP + g + 1)
                if n:
                    nc.scalar.mul(num[d][:, :], Y, hc[:, 2, c, d:d + 1]).then_inc(inter_ok, 1)
                if n < NT - 1:
                    act.wait_ge(c_f_ok, i * (NSTEP - 2) + g + 1)
                    nc.scalar.copy(c_st[d][0][:, :, :], c_f32[d][:, :, :]).then_inc(c_hi_ok, 1)

            act.wait_ge(raw_in, 16)
            nc.scalar.copy(w[0][0][:, :, :], w_raw[:, :, :]).then_inc(w_hi_ok, 1)
            with act.Fori(0, HEADS) as i:
                for t in range(NTILE):
                    n = t - FIRST_STEP_TILE
                    split(i, t + 1)
                    if t in (5, 6):
                        for g in range(3):
                            v_hi_part(i, t - 5, g)
                    evacuate(i, t, 0)
                    if 0 <= n < NT:
                        weights(i, n, 0)
                        weights(i, n, 1)
                        scores_hi(i, n, 0)
                        scores_hi(i, n, 1)
                    evacuate(i, t, 1)
                    if 0 <= n < NT:
                        after_state(i, n, 0)
                    evacuate(i, t, 2)
                    if KIND[t] == "conv_x":
                        tap1(i, t)
                    if 0 <= n < NT:
                        after_state(i, n, 1)

        @block.vector
        def _(dve):
            dve.wait_ge(const_ok, 1)
            for b in range(2):
                nc.vector.memset(buf[b][:, :], 0.0)
            nc.vector.memset(ones[:, :], 1.0)
            nc.vector.memset(f(ones_r[:, :]), 1.0)
            nc.vector.memset(f(v_hi[:, :, HD:HD + 2]), 1.0)
            nc.vector.memset(f(v_lo[:, :, HD:HD + 2]), 0.0).then_inc(const_ok, 1)
            dve.wait_ge(const_ok, 2)

            def split(i, t):
                b = t % 2
                dve.wait_ge(w_hi_ok, i * NTILE + t + 1)
                nc.vector.tensor_tensor(w[b][1][:, :, :], w_raw[:, :, :], f(w[b][0][:, :, :]), ALU.subtract).then_inc(w_ok, 1)

            HALF = {t: m for m, t in enumerate(t for t in range(NTILE) if KIND[t] in ("q", "k", "conv_z", "out_z"))}

            def evacuate(i, t, j):
                kind, (t0, n) = KIND[t], CHUNKS[j]
                src = pj[j][:, 0:n]
                if t in HALF:
                    dve.wait_ge(half, i * (3 * len(HALF)) + 3 * HALF[t] + j + 1)
                elif kind in ("conv_x", "conv_b"):
                    dve.wait_ge(pj_done, i * (3 * NTILE) + 3 * t + j + 1)
                if kind == "q":
                    nc.vector.tensor_tensor(q_lo[:, t, t0:t0 + n], src, f(q_hi[:, t, t0:t0 + n]), ALU.subtract).then_inc(pj_free_d, 1)
                elif kind == "k":
                    nc.vector.scalar_tensor_tensor(k_lo[:, t - 2, t0:t0 + n], src, K_SCALE, f(k_hi[:, t - 2, t0:t0 + n]),
                                                   ALU.mult, ALU.subtract).then_inc(pj_free_d, 1)
                elif kind == "conv_x":
                    m = A_TILES.index(t - 1)
                    dve.wait_ge(pj_free_a, i * (3 * len(A_TILES)) + 3 * m + j + 1)
                    nc.vector.tensor_tensor(span(buf[0], j), src, span(buf[0], j), ALU.mult).then_inc(pj_free_d, 1)
                elif kind == "conv_b":
                    dve.wait_ge(conv_tap, i * 6 + 3 * conv_pass(t) + 3)
                    nc.vector.tensor_tensor(span(buf[1], j), src, span(buf[1], j), ALU.mult).then_inc(pj_free_d, 1)
                elif kind in ("conv_z", "out_z"):
                    nc.vector.scalar_tensor_tensor(tan(t, j), tan(t, j), 1.0, src, ALU.add, ALU.mult).then_inc(pj_free_d, 1)
                    dve.wait_ge(pj_free_d, i * (3 * len(D_TILES)) + 3 * D_TILES.index(t) + j + 2)
                    if kind == "conv_z":
                        last = nc.vector.scalar_tensor_tensor(span(buf[1], j), tan(t, j), 0.5, span(buf[1], j), ALU.mult, ALU.mult)
                    else:
                        which = (t - 14) // 2
                        dve.wait_ge(pj_free_a, i * (3 * len(A_TILES)) + 3 * A_TILES.index(t - 1) + j + 1)
                        last = nc.vector.scalar_tensor_tensor(span(buf[which], j), span(buf[which], j), 1.0, tan(t, j), ALU.add, ALU.mult)
                    last.then_inc(gate_part, 1)
                    if kind == "conv_z" and j == 2:
                        dve.wait_ge(gate_part, i * 12 + {9: 3, 13: 6}[t] + 1)
                        dve.sem_inc(mix_ready, 1)

            def taps(i, t):
                j = conv_pass(t)
                dve.wait_ge(pj_free_d, i * (3 * len(D_TILES)) + 3 * D_TILES.index(t) + 4)
                dve.sem_inc(conv_tap, 1)
                inner = buf[1][:, 1:T + 3]
                dve.wait_ge(conv_mid, i * 4 + 2 * j + 1)
                nc.vector.scalar_tensor_tensor(inner, buf[0][:, 0:T + 2], conv_w[:, j, 0:1], inner, ALU.mult, ALU.add).then_inc(conv_tap, 1)
                dve.wait_ge(conv_tap, i * 6 + 3 * j + 2)
                nc.vector.scalar_tensor_tensor(inner, buf[0][:, 2:T + 4], conv_w[:, j, 2:3], inner, ALU.mult, ALU.add).then_inc(conv_tap, 1)
                dve.wait_ge(conv_tap, i * 6 + 3 * j + 3)
                dve.sem_inc(conv_mid, 1)
                dve.sem_inc(cw_used, 3)

            def v_lo_part(i, j, g):
                c0, nch = ((0, 2), (2, 4), (6, 4))[g]
                dve.wait_ge(vt_hi, i * 6 + 3 * j + g + 1)
                src = (x_bank, y_bank, z_bank)[g][:, 0:nch * P].rearrange("p (c e) -> p c e", e=P)
                dst = slice(j * P, (j + 1) * P)
                nc.vector.tensor_tensor(v_lo[:, c0:c0 + nch, dst], src, f(v_hi[:, c0:c0 + nch, dst]), ALU.subtract).then_inc(vt_ok, 1)

            def diagonal(i, n, d):
                c = n if d == 0 else BWD[n]
                nc.vector.tensor_scalar(diag[d][:, :], ident[:, :], hc[:, 1, c, d:d + 1], None, ALU.mult).then_inc(diag_ok, 1)

            def weigh(i, n, d):
                c, g = (n if d == 0 else BWD[n]), i * NSTEP + 2 * n + d + 1
                dve.wait_ge(wgt_ok, g)
                dve.wait_ge(kw_hi_ok, g)
                nc.vector.tensor_tensor(wgt[d][:, :], sek[d][:, 0:P], wgt[d][:, :], ALU.mult).then_inc(sw_f_ok, 1)
                nc.vector.scalar_tensor_tensor(kw[d][1][:, :], sek[d][:, 2 * P:4 * P], hc[:, 3, c, d:d + 1], f(kw[d][0][:, :]),
                                               ALU.mult, ALU.subtract).then_inc(kw_lo_ok, 1)

            def scores_lo(i, n, d):
                dve.wait_ge(sw_hi_ok, i * NSTEP + 2 * n + d + 1)
                nc.vector.tensor_tensor(sw[d][1][:, :], wgt[d][:, :], f(sw[d][0][:, :]), ALU.subtract).then_inc(sw_ok, 1)

            def after_state(i, n, d):
                c, g = (n if d == 0 else BWD[n]), i * NSTEP + 2 * n + d + 1
                dve.wait_ge(st_done, g)
                if n < NT - 1:
                    if n == 0:
                        nc.vector.tensor_copy(c_f32[d][:, :, HD:HD + 2], Y_n)
                        nc.vector.tensor_copy(c_f32[d][:, :, 0:HD], Z).then_inc(c_f_ok, 1)
                    else:
                        dve.wait_ge(inter_ok, i * (NSTEP - 2) + 2 * (n - 1) + d + 1)
                        for dst, new in ((slice(HD, HD + 2), Y_n), (slice(0, HD), Z)):
                            last = nc.vector.scalar_tensor_tensor(c_f32[d][:, :, dst], c_f32[d][:, :, dst], hc[:, 5, c, d:d + 1],
                                                                  new, ALU.mult, ALU.add)
                        last.then_inc(c_f_ok, 1)
                else:
                    dve.wait_ge(inter_ok, i * (NSTEP - 2) + 2 * (n - 1) + d + 1)
                if n:
                    nc.vector.tensor_tensor(num[d][:, :], X, num[d][:, :], ALU.add).then_inc(num_ok, 1)
                else:
                    nc.vector.tensor_copy(num[d][:, :], X).then_inc(num_ok, 1)
                dve.wait_ge(num_ok, g + 1)
                nc.vector.tensor_scalar(den[d][:, :], num[d][:, HD:HD + 1], -1.0, hc[:, 4, c, d:d + 1], ALU.mult, ALU.max).then_inc(den_ok, 1)
                if n < NT - 1:
                    dve.wait_ge(c_hi_ok, i * (NSTEP - 2) + 2 * n + d + 1)
                    nc.vector.tensor_tensor(c_st[d][1][:, :, :], c_f32[d][:, :, :], f(c_st[d][0][:, :, :]), ALU.subtract).then_inc(step_ok, 1)
                else:
                    dve.sem_inc(step_ok, 1)
                dve.wait_ge(den_ok, i * (2 * NSTEP) + 2 * (2 * n + d) + 1)
                nc.vector.tensor_tensor(den[d][:, :], num[d][:, HD:HD + 1], den[d][:, :], ALU.max).then_inc(den_ok, 1)
                dve.wait_ge(den_ok, i * (2 * NSTEP) + 2 * (2 * n + d) + 2)
                nc.vector.reciprocal(rec[d][:, :], den[d][:, :]).then_inc(rec_ok, 1)
                dve.wait_ge(rec_ok, g)
                other = BWD.index(c) if d == 0 else c
                if n < other or (n == other and d == 0):
                    nc.vector.tensor_scalar(h_tok[:, c, :], num[d][:, 0:HD], rec[d][:, :], None, ALU.mult).then_inc(h_ok, 1)
                else:
                    dve.wait_ge(h_ok, i * NSTEP + 2 * other + (1 - d) + 1)
                    nc.vector.scalar_tensor_tensor(h_tok[:, c, :], num[d][:, 0:HD], rec[d][:, :], h_tok[:, c, :], ALU.mult, ALU.add).then_inc(h_ok, 1)

            for free in (cw_used, gate_part, ht_used, step_ok, num_ok, pj_free_d):
                dve.sem_inc(free, 1)
            split(0, 0)
            with dve.Fori(0, HEADS) as i:
                for t in range(NTILE):
                    n = t - FIRST_STEP_TILE
                    split(i, t + 1)
                    if t in (5, 6):
                        for g in range(3):
                            v_lo_part(i, t - 5, g)
                    if n == -1:
                        dve.wait_ge(ht_used, i * 6 + 1)
                        nc.vector.tensor_copy(hc[:, :, :, :].rearrange("p q c d -> p (q c) d"),
                                              gate_col[:, :, :, :].rearrange("p q c (d h) -> p (q c) d h", d=2)[:, :, :, bass.ds(i, 1)].rearrange("p a d h -> p a (d h)")).then_inc(hc_ok, 1)
                        dve.wait_ge(hc_ok, i + 1)
                        diagonal(i, 0, 0)
                        diagonal(i, 0, 1)
                    evacuate(i, t, 0)
                    if 0 <= n < NT:
                        weigh(i, n, 0)
                        weigh(i, n, 1)
                        scores_lo(i, n, 0)
                        scores_lo(i, n, 1)
                        if n < NT - 1:
                            diagonal(i, n + 1, 0)
                            diagonal(i, n + 1, 1)
                    evacuate(i, t, 1)
                    if 0 <= n < NT:
                        after_state(i, n, 0)
                    evacuate(i, t, 2)
                    if KIND[t] == "conv_x":
                        taps(i, t)
                    if 0 <= n < NT:
                        after_state(i, n, 1)
                for j in range(2):
                    for g in range(3):
                        m = 3 * j + g
                        dve.wait_ge(ht, i * 6 + m + 1)
                        dve.wait_ge(gate_part, i * 12 + 13)
                        bank = [x_bank, y_bank, z_bank, sek[0], sek[1], x_bank][m]
                        nn = CHUNKS[g][1]
                        nc.vector.scalar_tensor_tensor(span(buf[j], g), span(buf[j], g), 0.25, bank[:, 0:nn], ALU.mult, ALU.mult).then_inc(ht_used, 1)
                    dve.wait_ge(ht_used, i * 6 + 3 * j + 4)
                    dve.sem_inc(mix_ready, 1)

        @block.tensor
        def _(pe):
            pe.wait_ge(const_ok, 2)

            def project(i, t, j):
                t0, n = CHUNKS[j]
                prev = (t - 1) % NTILE
                if KIND[prev] in BY_ACT:
                    sem, per, m = pj_free_a, 3 * len(A_TILES), A_TILES.index(prev)
                else:
                    sem, per, m = pj_free_d, 3 * len(D_TILES), D_TILES.index(prev)
                if t:
                    pe.wait_ge(sem, i * per + 3 * m + j + (1 if sem is pj_free_a else 2))
                else:
                    pe.wait_ge(sem, i * per + 1)
                for k in range(KD):
                    last = mm3(nc, pj[j][:, 0:n], (w[t % 2][0][:, k, :], w[t % 2][1][:, k, :]),
                               (u_hi[:, k, t0:t0 + n], u_lo[:, k, t0:t0 + n]), k == 0, k == KD - 1)
                last.then_inc(pj_done, 1)

            def v_transposes(i, j):
                for g, (c0, nch) in enumerate(((0, 2), (2, 4), (6, 4))):
                    if j:
                        pe.wait_ge(vt_ok, i * 6 + g + 1)
                    elif g == 0:
                        pe.wait_ge(ht_used, i * 6 + 1)
                        pe.wait_ge(pj_free_a, i * (3 * len(A_TILES)) + 3)
                    if j and g == 0:
                        pe.wait_ge(pj_free_a, i * (3 * len(A_TILES)) + 6)
                    bank = (x_bank, y_bank, z_bank)[g]
                    for c in range(nch):
                        col = (c0 + c) * P + (1 if c0 + c < NC else 3)
                        last = nc.tensor.transpose(bank[:, c * P:(c + 1) * P], buf[j][:, col:col + P], ident[:, :])
                    last.then_inc(vt, 1)

            def scores(i, n, d):
                c = n if d == 0 else BWD[n]
                t0 = c * P
                if n == 0:
                    pe.wait_ge(ht_used, i * 6 + 1)
                    pe.wait_ge(pj_free_d, i * (3 * len(D_TILES)) + 13)
                pe.wait_ge(diag_ok, i * NSTEP + 2 * n + d + 1)
                bank = sek[d]
                for j in range(2):
                    mm3(nc, bank[:, 0:P], (k_hi[:, j, t0:t0 + P], k_lo[:, j, t0:t0 + P]), (q_hi[:, j, t0:t0 + P], q_lo[:, j, t0:t0 + P]), j == 0, j == 1)
                nc.tensor.matmul(bank[:, P:2 * P], ones[:, :], diag[d][:, :], start=True, stop=False)
                nc.tensor.matmul(bank[:, P:2 * P], ident_b[:, :], mask[:, d, :], start=False, stop=True)
                for j in range(2):
                    nc.tensor.matmul(bank[:, (2 + j) * P:(3 + j) * P], k_hi[:, j, t0:t0 + P], ident_r[:, :], start=True, stop=False)
                    last = nc.tensor.matmul(bank[:, (2 + j) * P:(3 + j) * P], k_lo[:, j, t0:t0 + P], ident_r[:, :], start=False, stop=True)
                last.then_inc(sc_done, 1)

            def state(i, n, d):
                c, g = (n if d == 0 else BWD[n]), 2 * n + d
                t0 = c * P
                if n == 0 and d == 0:
                    pe.wait_ge(vt_ok, i * 6 + 6)
                pe.wait_ge(step_ok, i * NSTEP + g + 1)
                pe.wait_ge(num_ok, i * NSTEP + g + 1)
                if n:
                    for j in range(2):
                        last = mm3(nc, Y, (q_hi[:, j, t0:t0 + P], q_lo[:, j, t0:t0 + P]), (c_st[d][0][:, j, :], c_st[d][1][:, j, :]), j == 0, j == 1)
                pe.wait_ge(kw_lo_ok, i * NSTEP + g + 1)
                if n < NT - 1:
                    for j in range(2):
                        kj = slice(j * P, (j + 1) * P)
                        mm3(nc, Z[:, j, :], (kw[d][0][:, kj], kw[d][1][:, kj]), (v_hi[:, c, 0:HD], v_lo[:, c, 0:HD]))
                        nc.tensor.matmul(Y_n[:, j, :], kw[d][0][:, kj], ones_r[:, :], start=True, stop=False)
                        nc.tensor.matmul(Y_n[:, j, :], kw[d][1][:, kj], ones_r[:, :], start=False, stop=True)
                pe.wait_ge(sw_ok, i * NSTEP + g + 1)
                mm3(nc, X, (sw[d][0][:, :], sw[d][1][:, :]), (v_hi[:, c, :], v_lo[:, c, :])).then_inc(st_done, 1)

            with pe.Fori(0, HEADS) as i:
                for t in range(NTILE):
                    n = t - FIRST_STEP_TILE
                    pe.wait_ge(w_ok, i * NTILE + t + 1)
                    project(i, t, 0)
                    if 0 <= n < NT:
                        scores(i, n, 0)
                        scores(i, n, 1)
                    project(i, t, 1)
                    if t in (5, 6):
                        v_transposes(i, t - 5)
                    if 0 <= n < NT:
                        state(i, n, 0)
                    project(i, t, 2)
                    if 0 <= n < NT:
                        state(i, n, 1)
                for j in range(2):
                    for g, (c0, nch) in enumerate(((0, 2), (2, 4), (6, 4))):
                        m = 3 * j + g
                        if m == 0:
                            pe.wait_ge(step_ok, i * NSTEP + NSTEP + 1)
                            pe.wait_ge(num_ok, i * NSTEP + NSTEP + 1)
                            pe.wait_ge(h_ok, i * NSTEP + NSTEP)
                        if m == 5:
                            pe.wait_ge(ht_used, i * 6 + 2)
                        bank = [x_bank, y_bank, z_bank, sek[0], sek[1], x_bank][m]
                        for c in range(nch):
                            last = nc.tensor.transpose(bank[:, c * P:(c + 1) * P], h_tok[:, c0 + c, j * P:(j + 1) * P], ident[:, :])
                        last.then_inc(ht, 1)


def stage_out(nc, a, keep, layer):
    H = KM // 2
    ident, mod_col = keep["ident"], keep["mod_col"]
    tiles = NT if layer == 0 else LAT // P
    src = (a["mixT"] if layer == 0 else a["ogT"]).rearrange("(k p) t -> p k t", p=P)
    resid = (a["h0"] if layer == 0 else a["h1"]).rearrange("(n p) d -> n p d", p=P)
    result = (a["h1"] if layer == 0 else a["out"]).rearrange("(n p) d -> n p d", p=P)
    u_dst = a["u1T"].rearrange("(k p) t -> p k t", p=P)
    w_src = a["ev_w_out" if layer == 0 else "od_w_out"].rearrange("a (k p) n -> k p (a n)", p=P)
    with ExitStack() as ctx:
        s = Space(nc, ctx, f"o{layer}")
        w_hi, w_lo = s.pair("w", [P, KM, D])
        w_raw = [s.sb(f"w_raw{i}", [P, D]) for i in range(2)]
        m_raw = [s.sb(f"m_raw{i}", [P, H, P]) for i in range(2)]
        m = [s.pair(f"m{i}", [P, H, P]) for i in range(2)]
        res = [s.sb(f"res{i}", [P, D]) for i in range(2)]
        y = [s.sb(f"y{i}", [P, D]) for i in range(2)]
        u_out = [s.sb(f"u_out{i}", [P, KD, P]) for i in range(2)] if layer == 0 else None
        g_bc = {v: s.sb(f"g_bc{v}", [P, D]) for v in ((0, 1) if layer == 0 else (0,))}
        ln_g, ln_b = s.sb("ln_g", [P, D]), s.sb("ln_b", [P, D])
        stats, mean_var = s.sb("stats", [P, 2, 6]), s.sb("mean_var", [P, 2])
        rstd, minus_half, eps = s.sb("rstd", [P, 1]), s.sb("minus_half", [P, 1]), s.sb("eps", [P, 1])
        y_bank = [s.bank(f"y_bank{i}", 2) for i in range(2)]
        t_bank = [s.bank(f"t_bank{i}") for i in range(2)]
        w_in = [s.sem(f"w_in{i}") for i in range(2)]
        m_in = [s.sem(f"m_in{i}") for i in range(2)]
        res_in = [s.sem(f"res_in{i}") for i in range(2)]
        rows_in, w_hi_ok, w_ok, m_hi_ok, m_ok = (s.sem(n) for n in ("rows_in", "w_hi_ok", "w_ok", "m_hi_ok", "m_ok"))
        y_half, y_read, res_used, sum_ok, stats_ok, mv_ok, var_ok, rstd_ok, norm_ok, gain_ok, ln_ok = (s.sem(n) for n in (
            "y_half", "y_read", "res_used", "sum_ok", "stats_ok", "mv_ok", "var_ok", "rstd_ok", "norm_ok", "gain_ok", "ln_ok"))
        tr_done, tr_used = s.sem("tr_done"), s.sem("tr_used")
        half_ok, stats_seen = s.sem("half_ok"), s.sem("stats_seen")
        y_out = [s.sem(f"y_out{i}") for i in range(2)]
        u_stored = [s.sem(f"u_stored{i}") for i in range(2)]
        block = ctx.enter_context(nc.Block())
        SPANS = [(0, 1, 1), (1, tiles // 2, 0)] if layer == 0 else [(0, 1, 0), (1, tiles // 2, 0)]

        def pairs(eng, body):
            for lo, hi, v in SPANS:
                if hi - lo == 1:
                    for b in range(2):
                        body(lo, b, v, True)
                else:
                    with eng.Fori(lo, hi) as i:
                        for b in range(2):
                            body(i, b, v, False)

        @block.sync
        def _(sp):
            sp.dma_start(m_raw[0][:, :, :], src[:, 0:H, 0:P]).then_inc(m_in[0], 16)
            sp.dma_start(m_raw[1][:, :, :], src[:, H:KM, 0:P]).then_inc(m_in[1], 16)
            for k in range(KM):
                if k >= 2:
                    sp.wait_ge(w_ok, k - 1)
                sp.dma_start(w_raw[k % 2][:, :], w_src[k]).then_inc(w_in[k % 2], 16)

            def tile(i, b, v, peeled):
                first = peeled and b == 0
                tok = i * (2 * P) + b * P if peeled else sp.snap(i * (2 * P) + b * P)
                n = i * 2 + b if peeled else sp.snap(i * 2 + b)
                n2 = n * 2 if peeled else sp.snap(i * 4 + 2 * b)
                for h in range(2):
                    if not first:
                        sp.wait_ge(m_ok, n2 + (h + 1))
                        sp.dma_start(m_raw[h][:, :, :], src[:, H * h:H * h + H, bass.ds(tok, P)]).then_inc(m_in[h], 16)
                sp.wait_ge(res_used, n + 1)
                sp.dma_start(res[b][:, :], resid[bass.ds(n, 1)].rearrange("n p d -> (n p) d")).then_inc(res_in[b], 16)
            pairs(sp, tile)

        @block.gpsimd
        def _(pool):
            for v, t in g_bc.items():
                pool.dma_start(t[:, :], a["g_rows"][layer, v:v + 1, :].partition_broadcast(P)).then_inc(rows_in, 16)
            pool.dma_start(ln_g[:, :], a["ln_g"][layer:layer + 1, :].partition_broadcast(P)).then_inc(rows_in, 16)
            pool.dma_start(ln_b[:, :], a["ln_b"][layer:layer + 1, :].partition_broadcast(P)).then_inc(rows_in, 16)
            pool.memset(eps[:, :], LN_EPS).then_inc(half_ok, 1)
            pool.memset(minus_half[:, :], -0.5).then_inc(half_ok, 1)
            pool.wait_ge(half_ok, 2)
            pool.wait_ge(rows_in, 16 * (2 + len(g_bc)))

            def tile(i, b, v, peeled):
                n = i * 2 + b if peeled else pool.snap(i * 2 + b)
                pool.wait_ge(mv_ok, n + 1)
                pool.tensor_tensor(rstd[:, :], mean_var[:, 1:2], eps[:, :], ALU.add).then_inc(var_ok, 1)
                pool.wait_ge(var_ok, n + 1)
                pool.tensor_tensor(rstd[:, :], rstd[:, :], minus_half[:, :], ALU.pow).then_inc(rstd_ok, 1)
                pool.wait_ge(norm_ok, n + 1)
                pool.tensor_tensor(y[b][:, :], y[b][:, :], ln_g[:, :], ALU.mult).then_inc(gain_ok, 1)
                pool.wait_ge(gain_ok, n + 1)
                pool.tensor_tensor(y[b][:, :], y[b][:, :], ln_b[:, :], ALU.add).then_inc(ln_ok, 1)
                if layer == 1 or v == 0:
                    pool.wait_ge(ln_ok, n + 1)
                    row = n - NC if layer == 0 else n
                    pool.dma_start(result[bass.ds(row, 1)].rearrange("n p d -> (n p) d"), y[b][:, :]).then_inc(y_out[b], 16)
            pairs(pool, tile)
            for b in range(2):
                pool.wait_ge(y_out[b], 16 * (LAT // P // 2))

        @block.scalar
        def _(act):
            def split(i, b):
                n = i * 2 + b
                for h in range(2):
                    act.wait_ge(m_in[h], n * 16 + 16)
                    act.wait_ge(y_half, n * 2 + (h + 1))
                    nc.scalar.copy(m[h][0][:, :, :], m_raw[h][:, :, :]).then_inc(m_hi_ok, 1)

            def modulate(i, b, v):
                n = i * 2 + b
                act.wait_ge(u_stored[b], i * 16)
                for k in range(KD):
                    if k % 4 == 0:
                        act.wait_ge(tr_done, n * 2 + (k // 4 + 1))
                    last = nc.scalar.activation(u_out[b][:, k, :], t_bank[k // 4][:, (k % 4) * P:(k % 4 + 1) * P], ACT.Identity,
                                                scale=mod_col[:, 1, KD + k, v:v + 1], bias=mod_col[:, 1, k, v:v + 1])
                    if k % 4 == 3:
                        last.then_inc(tr_used, 1)
                act.wait_ge(tr_used, n * 2 + 2)
                tok = i * (2 * P) + b * P
                act.dma_start(u_dst[:, :, bass.ds(tok, P)], u_out[b][:, :, :]).then_inc(u_stored[b], 16)

            split(0, 0)
            for k in range(KM):
                act.wait_ge(w_in[k % 2], 16 * (k // 2 + 1))
                nc.scalar.copy(w_hi[:, k, :], w_raw[k % 2][:, :]).then_inc(w_hi_ok, 1)

            if layer == 0:
                split(0, 1)
                modulate(0, 0, 1)
                split(1, 0)
                modulate(0, 1, 1)
                split(1, 1)
                modulate(1, 0, 0)
                with act.Fori(2, tiles // 2) as i:
                    split(i, 0)
                    modulate(i - 1, 1, 0)
                    split(i, 1)
                    modulate(i, 0, 0)
                modulate(tiles // 2 - 1, 1, 0)
                for b in range(2):
                    act.wait_ge(u_stored[b], 16 * (tiles // 2))
            else:
                split(0, 1)
                with act.Fori(1, tiles // 2) as i:
                    split(i, 0)
                    split(i, 1)

        @block.vector
        def _(dve):
            dve.sem_inc(m_ok, 2)
            dve.sem_inc(y_half, 2)
            dve.sem_inc(y_read, 2)
            dve.sem_inc(res_used, 2)

            def split(i, b):
                n = i * 2 + b
                for h in range(2):
                    dve.wait_ge(m_hi_ok, n * 2 + (h + 1))
                    nc.vector.tensor_tensor(m[h][1][:, :, :], m_raw[h][:, :, :], f(m[h][0][:, :, :]), ALU.subtract).then_inc(m_ok, 1)

            def norm(i, b, v):
                n = i * 2 + b
                dve.wait_ge(y_half, n * 2 + 4)
                if layer == 0:
                    if not isinstance(n, int) or n >= 2:
                        dve.wait_ge(tr_done, n * 2 - 2)
                    if v == 0 and (not isinstance(i, int) or i >= 2):
                        dve.wait_ge(y_out[b], (i - 1) * 16)
                else:
                    dve.wait_ge(y_out[b], i * 16)
                nc.vector.tensor_tensor(y[b][:, :], y_bank[b][:, :], g_bc[v][:, :], ALU.mult).then_inc(y_read, 1)
                dve.wait_ge(y_read, n + 3)
                dve.wait_ge(res_in[b], i * 16 + 16)
                nc.vector.scalar_tensor_tensor(y[b][:, :], res[b][:, :], ALPHA, y[b][:, :], ALU.mult, ALU.add).then_inc(res_used, 1)
                dve.wait_ge(res_used, n + 3)
                for h in range(2):
                    last = nc.vector.bn_stats(stats[:, h, :], y[b][:, 512 * h:512 * h + 512])
                last.then_inc(stats_ok, 1)
                dve.wait_ge(stats_ok, n + 1)
                dve.sem_inc(stats_seen, 1)
                nc.vector.bn_aggr(mean_var[:, :], stats[:, :, :]).then_inc(mv_ok, 1)

            def scale(i, b):
                n = i * 2 + b
                dve.wait_ge(rstd_ok, n + 1)
                nc.vector.tensor_scalar(y[b][:, :], y[b][:, :], mean_var[:, 0:1], rstd[:, :], ALU.subtract, ALU.mult).then_inc(norm_ok, 1)

            split(0, 0)
            for k in range(KM):
                dve.wait_ge(w_hi_ok, k + 1)
                nc.vector.tensor_tensor(w_lo[:, k, :], w_raw[k % 2][:, :], f(w_hi[:, k, :]), ALU.subtract).then_inc(w_ok, 1)
            dve.wait_ge(rows_in, 16 * (2 + len(g_bc)))
            split(0, 1)
            norm(0, 0, SPANS[0][2])
            scale(0, 0)
            split(1, 0)
            norm(0, 1, SPANS[0][2])
            scale(0, 1)
            split(1, 1)
            norm(1, 0, 0)
            scale(1, 0)
            with dve.Fori(2, tiles // 2) as i:
                split(i, 0)
                norm(i - 1, 1, 0)
                scale(i - 1, 1)
                split(i, 1)
                norm(i, 0, 0)
                scale(i, 0)
            norm(tiles // 2 - 1, 1, 0)
            scale(tiles // 2 - 1, 1)

        @block.tensor
        def _(pe):
            def project(i, b, h, peeled=False):
                n = i * 2 + b
                pe.wait_ge(m_ok, n * 2 + (h + 3))
                if h == 0:
                    pe.wait_ge(y_read, n + 1)
                for k in range(H):
                    if peeled and b == 0:
                        pe.wait_ge(w_ok, H * h + k + 1)
                    for o in range(2):
                        cols = slice(512 * o, 512 * o + 512)
                        last = mm3(nc, y_bank[b][:, cols], (m[h][0][:, k, :], m[h][1][:, k, :]),
                                   (w_hi[:, H * h + k, cols], w_lo[:, H * h + k, cols]), h == 0 and k == 0, h == 1 and k == H - 1)
                last.then_inc(y_half, 1)

            def transposes(i, b):
                n = i * 2 + b
                pe.wait_ge(ln_ok, n + 1)
                pe.wait_ge(tr_used, n * 2)
                for g in range(2):
                    for k in range(4):
                        kk = 4 * g + k
                        last = nc.tensor.transpose(t_bank[g][:, k * P:(k + 1) * P], y[b][:, kk * P:(kk + 1) * P], ident[:, :])
                    last.then_inc(tr_done, 1)

            project(0, 0, 0, True)
            project(0, 0, 1, True)
            project(0, 1, 0)
            if layer == 0:
                transposes(0, 0)
            project(0, 1, 1)
            project(1, 0, 0)
            if layer == 0:
                transposes(0, 1)
            project(1, 0, 1)
            project(1, 1, 0)
            if layer == 0:
                transposes(1, 0)
            project(1, 1, 1)
            with pe.Fori(2, tiles // 2) as i:
                project(i, 0, 0)
                if layer == 0:
                    transposes(i - 1, 1)
                project(i, 0, 1)
                project(i, 1, 0)
                if layer == 0:
                    transposes(i, 0)
                project(i, 1, 1)
            if layer == 0:
                transposes(tiles // 2 - 1, 1)


def stage_latent(nc, a, keep):
    lq, lkv, kr2, rope = keep["lq"], keep["lkv"], keep["kr2"], keep["rope"]
    TILES = [("q", j, P * j, P) for j in range(3)] + [("kv", j, QR + P * j, P) for j in range(2)] + [("kr", 0, QR + KVR, DR)]
    Z0 = QR + KVR + DR
    NL = len(TILES)
    chunks = lambda kind: (1, 2) if kind in ("q", "z") else (0, 1, 2)
    WORK = [(t, j) for t, (kind, *_) in enumerate(TILES) for j in chunks(kind)]
    at = {tj: n for n, tj in enumerate(WORK)}
    SQ = [tj for tj in WORK if TILES[tj[0]][0] != "kr"]
    with ExitStack() as ctx:
        s = Space(nc, ctx, "l")
        u_hi, u_lo = s.pair("u", [P, KD, T])
        u_raw = [s.sb(f"u_raw{i}", [P, T]) for i in range(2)]
        w_raw = s.sb("w_raw", [P, KD, P])
        w = [s.pair(f"w{i}", [P, KD, P]) for i in range(2)]
        lat = s.sb("lat", [P, 3, LAT])
        lat_kv = lat[:, :, :].rearrange("p a t -> p (a t)")[:, 0:2 * T].rearrange("p (a t) -> p a t", a=2)
        sq = [s.sb(f"sq{i}", [P, 512]) for i in range(2)]
        rms = s.sb("rms", [P, T])
        kr = s.sb("kr", [DR, T])
        ones = s.sb("ones", [P, P])
        eps = s.sb("eps", [P, 1])
        q_gain, kv_gain = s.sb("q_gain", [P, 3]), s.sb("kv_gain", [P, 2])
        pj = [s.bank(f"pj{j}") for j in range(3)]
        ss = [s.bank(f"ss{j}") for j in range(3)]
        u_in = [s.sem(f"u_in{i}") for i in range(2)]
        w_in, const_in, zero_ok = s.sem("w_in"), s.sem("const_in"), s.sem("zero_ok")
        u_hi_ok, u_ok, w_hi_ok, w_ok, pj_done, sq_ok, lat_ok, ss_done = (s.sem(n) for n in (
            "u_hi_ok", "u_ok", "w_hi_ok", "w_ok", "pj_done", "sq_ok", "lat_ok", "ss_done"))
        ms_ok, rms_ok, n_ok, n_hi_ok, n_lo_ok, kr_step, kr_hi_ok, kr_lo_ok = (s.sem(n) for n in (
            "ms_ok", "rms_ok", "n_ok", "n_hi_ok", "n_lo_ok", "kr_step", "kr_hi_ok", "kr_lo_ok"))
        z_stored, z_done, z_tanh, z_ok = s.sem("z_stored"), s.sem("z_done"), s.sem("z_tanh"), s.sem("z_ok")
        z_out = [s.sem(f"z_out{i}") for i in range(2)]
        w_src = a["od_w_in"].rearrange("a (k p) n -> p (a k) n", p=P)
        u_src = a["u1T"].rearrange("(k p) t -> k p t", p=P)
        zg_dst = a["zgT"].rearrange("(j p) t -> j p t", p=P)
        zt = lambda b, h: lat[:, b, 512 * h:512 * h + 512]
        block = ctx.enter_context(nc.Block())

        @block.sync
        def _(sp):
            for k in range(KD):
                if k >= 2:
                    sp.wait_ge(u_ok, k - 1)
                sp.dma_start(u_raw[k % 2][:, :], u_src[k]).then_inc(u_in[k % 2], 16)
                if k == 1:
                    sp.dma_start(w_raw[:, :, :], w_src[:, :, 0:P]).then_inc(w_in, 16)
                    sp.dma_start(q_gain[:, :], a["od_q_norm"]).then_inc(const_in, 16)
                    sp.dma_start(kv_gain[:, :], a["od_kv_norm"]).then_inc(const_in, 16)
                    sp.dma_start(rope[:, :, :], a["c_rope"].rearrange("c r t -> r c t")).then_inc(const_in, 16)
            for t in range(1, NL):
                _, _, col, n = TILES[t]
                sp.wait_ge(w_ok, t)
                sp.dma_start(w_raw[:, :, 0:n], w_src[:, :, col:col + n]).then_inc(w_in, 16)
            with sp.Fori(0, AH // 2) as i:
                for b in range(2):
                    sp.wait_ge(w_ok, i * 2 + (NL + b))
                    sp.dma_start(w_raw[:, :, :], w_src[:, :, bass.ds(i * (2 * P) + (Z0 + P * b), P)]).then_inc(w_in, 16)

        @block.scalar
        def _(act):
            def split(t, i=None):
                if i is None:
                    act.wait_ge(w_in, 16 * (t + 1))
                    if t >= 2:
                        act.wait_ge(pj_done, at[(t - 2, 2)] + 1)
                    n = TILES[t][3]
                else:
                    act.wait_ge(w_in, i * 32 + 16 * (t + 1))
                    act.wait_ge(z_done, i * 4 + 2 * (t - NL) + 1)
                    n = P
                nc.scalar.copy(w[t % 2][0][:, :, 0:n], w_raw[:, :, 0:n]).then_inc(w_hi_ok, 1)

            def inverse_rms(group, width, js):
                act.wait_ge(ss_done, max(SQ.index(tj) for tj in SQ if TILES[tj[0]][0] == group) + 1)
                if group == "kv":
                    act.wait_ge(n_ok, 3)
                for j in js:
                    t0, n = CHUNKS[j]
                    nc.scalar.activation(rms[:, t0:t0 + n], ss[j][:, 0:n], ACT.Ln, scale=1.0 / width, bias=eps[:, :]).then_inc(ms_ok, 1)
                act.wait_ge(ms_ok, 2 if group == "q" else 5)
                t0 = CTX if group == "q" else 0
                nc.scalar.activation(rms[:, t0:T], rms[:, t0:T], ACT.Exp, scale=-0.5).then_inc(rms_ok, 1)

            for k in range(KD):
                act.wait_ge(u_in[k % 2], 16 * (k // 2 + 1))
                nc.scalar.copy(u_hi[:, k, :], u_raw[k % 2][:, :]).then_inc(u_hi_ok, 1)
                if k == 1:
                    split(0)
            for t, (kind, f_, _, _) in enumerate(TILES):
                if t + 1 < NL:
                    split(t + 1)
                if kind == "kv" and f_ == 0:
                    act.wait_ge(n_lo_ok, 3)
                for j in chunks(kind):
                    t0, n = CHUNKS[j]
                    act.wait_ge(pj_done, at[(t, j)] + 1)
                    if kind == "kr":
                        nc.scalar.copy(kr[:, t0:t0 + n], pj[j][0:DR, 0:n]).then_inc(lat_ok, 1)
                        continue
                    m = SQ.index((t, j))
                    if m >= 2:
                        act.wait_ge(ss_done, m - 1)
                    nc.scalar.activation(sq[m % 2][:, 0:n], pj[j][:, 0:n], ACT.Square).then_inc(sq_ok, 1)
                    dst = lat[:, f_, t0 - CTX:t0 - CTX + n] if kind == "q" else lat_kv[:, f_, t0:t0 + n]
                    nc.scalar.copy(dst, pj[j][:, 0:n]).then_inc(lat_ok, 1)
                if kind == "q" and f_ == 2:
                    act.wait_ge(zero_ok, 2)
                    inverse_rms("q", QR, (1, 2))
                    for x in range(3):
                        act.wait_ge(n_ok, x + 1)
                        nc.scalar.copy(lq[0][:, x, :], lat[:, x, :]).then_inc(n_hi_ok, 1)
            inverse_rms("kv", KVR, (0, 1, 2))
            for x in range(2):
                act.wait_ge(n_ok, 4 + x)
                nc.scalar.copy(lkv[0][:, x, :], lat_kv[:, x, :]).then_inc(n_hi_ok, 1)
            act.wait_ge(kr_step, 4)
            for r in range(2):
                nc.scalar.copy(kr2[0][DR * r:DR * r + DR, :], kr[:, :]).then_inc(kr_hi_ok, 1)
            act.wait_ge(pj_done, len(WORK))
            act.wait_ge(n_lo_ok, 5)
            with act.Fori(0, AH // 2) as i:
                split(NL, i)
                for b in range(2):
                    if b == 0:
                        split(NL + 1, i)
                    act.wait_ge(z_stored, i * 2 + (b + 1))
                    for h in range(2):
                        act.wait_ge(z_done, i * 4 + (2 * b + h + 3) + 1)
                        nc.scalar.activation(zt(b, h), pj[h + 1][:, :], ACT.Tanh, scale=0.5).then_inc(z_tanh, 1)

        @block.gpsimd
        def _(pool):
            pool.memset(eps[:, :], RMS_EPS).then_inc(zero_ok, 1)
            pool.sem_inc(z_stored, 2)
            with pool.Fori(0, AH // 2) as i:
                for b in range(2):
                    pool.wait_ge(z_ok, i * 4 + (2 * b + 2) + 1)
                    pool.dma_start(zg_dst[bass.ds(i * 2 + b, 1)].rearrange("j p t -> (j p) t"), lat[:, b, :]).then_inc(z_out[b], 16)
                    pool.wait_ge(z_out[b], i * 16 + 16)
                    pool.sem_inc(z_stored, 1)

        @block.vector
        def _(dve):
            nc.vector.memset(ones[:, :], 1.0).then_inc(zero_ok, 1)

            def split(t, i=None):
                n = TILES[t][3] if i is None else P
                dve.wait_ge(w_hi_ok, t + 1 if i is None else i * 2 + (t + 1))
                nc.vector.tensor_tensor(w[t % 2][1][:, :, 0:n], w_raw[:, :, 0:n], f(w[t % 2][0][:, :, 0:n]), ALU.subtract).then_inc(w_ok, 1)

            def normalise(group):
                src, gain, (hi, lo), x0 = (lat, q_gain, lq, 0) if group == "q" else (lat_kv, kv_gain, lkv, 3)
                r0 = CTX if group == "q" else 0
                tiles = 3 if group == "q" else 2
                dve.wait_ge(rms_ok, 1 if group == "q" else 2)
                dve.wait_ge(lat_ok, max(at[tj] for tj in WORK if TILES[tj[0]][0] == group) + 1)
                for x in range(tiles):
                    nc.vector.scalar_tensor_tensor(src[:, x, :], src[:, x, :], gain[:, x:x + 1], rms[:, r0:T], ALU.mult, ALU.mult).then_inc(n_ok, 1)
                for x in range(tiles):
                    dve.wait_ge(n_hi_ok, x0 + x + 1)
                    nc.vector.tensor_tensor(lo[:, x, :], src[:, x, :], f(hi[:, x, :]), ALU.subtract).then_inc(n_lo_ok, 1)

            for k in range(KD):
                dve.wait_ge(u_hi_ok, k + 1)
                nc.vector.tensor_tensor(u_lo[:, k, :], u_raw[k % 2][:, :], f(u_hi[:, k, :]), ALU.subtract).then_inc(u_ok, 1)
                if k == 1:
                    split(0)
            for t in range(1, 4):
                split(t)
            dve.wait_ge(const_in, 48)
            normalise("q")
            split(4)
            split(5)
            normalise("kv")
            dve.wait_ge(lat_ok, len(WORK))
            dve.wait_ge(u_ok, KD)
            part = [u_raw[x][0:DR, 0:LAT] for x in range(2)]
            HR = DR // 2
            nc.vector.tensor_tensor(part[0], kr[:, CTX:T], rope[:, 0, :], ALU.mult)
            for r in range(2):
                o = 1 - r
                nc.vector.tensor_tensor(part[1][HR * r:HR * r + HR, :], kr[HR * o:HR * o + HR, CTX:T], rope[HR * o:HR * o + HR, 1, :], ALU.mult)\
                    .then_inc(kr_step, 1 + r)
            dve.wait_ge(kr_step, 3)
            nc.vector.tensor_tensor(kr[:, CTX:T], part[0], part[1], ALU.add).then_inc(kr_step, 1)
            for r in range(2):
                dve.wait_ge(kr_hi_ok, 2)
                nc.vector.tensor_tensor(kr2[1][DR * r:DR * r + DR, :], kr[:, :], f(kr2[0][0:DR, :]), ALU.subtract).then_inc(kr_lo_ok, 1)
            dve.sem_inc(z_ok, 1)
            with dve.Fori(0, AH // 2) as i:
                split(NL, i)
                for b in range(2):
                    if b == 0:
                        split(NL + 1, i)
                    for h in range(2):
                        dve.wait_ge(z_tanh, i * 4 + (2 * b + h + 1))
                        nc.vector.scalar_tensor_tensor(zt(b, h), zt(b, h), 1.0, pj[h + 1][:, :], ALU.add, ALU.mult).then_inc(z_ok, 1)

        @block.tensor
        def _(pe):
            def project(out, t, j, n, waits=False):
                t0, cols = CHUNKS[j]
                for k in range(KD):
                    if waits:
                        pe.wait_ge(u_ok, k + 1)
                    last = mm3(nc, out, (w[t % 2][0][:, k, 0:n], w[t % 2][1][:, k, 0:n]),
                               (u_hi[:, k, t0:t0 + cols], u_lo[:, k, t0:t0 + cols]), k == 0, k == KD - 1)
                return last

            def sum_squares(m):
                t, j = SQ[m]
                kind, f_ = TILES[t][:2]
                n = CHUNKS[j][1]
                pe.wait_ge(sq_ok, m + 1)
                if kind == "kv" and f_ == 0 and j:
                    pe.wait_ge(ms_ok, 2)
                nc.tensor.matmul(ss[j][:, 0:n], ones[:, :], sq[m % 2][:, 0:n], start=f_ == 0,
                                 stop=f_ == (2 if kind == "q" else 1)).then_inc(ss_done, 1)

            pe.wait_ge(zero_ok, 2)
            for m, (t, j) in enumerate(WORK):
                kind, _, _, n = TILES[t]
                if j == chunks(kind)[0]:
                    pe.wait_ge(w_ok, t + 1)
                if t and (t - 1, j) in at:
                    pe.wait_ge(lat_ok, at[(t - 1, j)] + 1)
                project(pj[j][0:n, 0:CHUNKS[j][1]], t, j, n, waits=m == 0).then_inc(pj_done, 1)
                if 1 <= m <= len(SQ):
                    sum_squares(m - 1)
            pe.wait_ge(lat_ok, len(WORK))
            pe.sem_inc(z_done, 3)
            with pe.Fori(0, AH // 2) as i:
                for b in range(2):
                    pe.wait_ge(w_ok, i * 2 + (NL + b + 1))
                    for h in range(2):
                        pe.wait_ge(z_ok, i * 4 + (2 * b + 1))
                        project(pj[h + 1][:, :], NL + b, h + 1, P).then_inc(z_done, 1)


def stage_attend(nc, a, keep):
    lq, lkv, kr2, rope, ident = keep["lq"], keep["lkv"], keep["kr2"], keep["rope"], keep["ident"]
    QT = LAT // P
    KEYS = [(0, 512), (512, 512), (1024, 256)]
    KTILES = [(0, 4), (4, 4), (8, 2)]
    VTILES = [(0, 4), (4, 4), (8, 2)]
    PROJ = {0: (("qn", 0), ("qn", 1)), 1: (("qr", 0), ("qr", 1)), 2: (None, None), 3: (("kn", 0), None),
            4: (("kn", 1), ("kn", 2)), 5: (("v", 0), None), 6: (("v", 1), None), 7: (("v", 2), None)}
    WQ_SLOT, WK_SLOT, QS_SLOT = 3, 7, 2

    def slot_ops(t):
        first, second = PROJ[t]
        ops = [[("T", (t - 2) % QT, 0)], [("T", (t - 2) % QT, 1)], [("T", (t - 2) % QT, 2)]]
        if t in (2, 6):
            ops[0].insert(0, ("PV", 1 if t == 2 else 0))
        if first:
            ops[1].append(first)
        if second:
            ops[2].append(second)
        return ops

    SEQ = [op for t in range(QT) for part in slot_ops(t) for op in part]
    NEW = ("qn", "qr", "kn", "v")
    PROLOGUE = [op for op in SEQ if op[0] in NEW]
    OLD = [op for t in range(3) for part in slot_ops(t) for op in part
           if (op[0] == "T" and t < 2) or op == ("PV", 1)]
    TAIL = [("T", 6, 0), ("T", 6, 1), ("T", 6, 2), ("T", 7, 0), ("T", 7, 1), ("T", 7, 2), ("PV", 1)]
    SEQ_FIRST = [op for op in SEQ if op not in OLD]
    SEQ_LAST = [op for op in SEQ if op[0] not in NEW]

    def order(part, i, b, op, ops=lambda op: True, c=0):
        count = lambda seq: sum(1 for o in seq if ops(o))
        upto = lambda seq: count(seq[:seq.index(op) + 1])
        if part == "prologue":
            return upto(PROLOGUE) + c
        if part == "first" and b == 0:
            return count(PROLOGUE) + upto(SEQ_FIRST) + c
        before = count(PROLOGUE) - count(OLD)
        if part == "tail":
            return before + (AH - 1) * count(SEQ) + count(SEQ_LAST) + upto(TAIL) + c
        seq = SEQ_LAST if part == "last" and b == 1 else SEQ
        return i * (2 * count(SEQ)) + (b * count(SEQ) + before + upto(seq) + c)

    has_hi = lambda op: op[0] in ("T", "qn", "kn", "v")

    with ExitStack() as ctx:
        s = Space(nc, ctx, "t")
        qn = [s.pair(f"qn{b}", [P, LAT]) for b in range(2)]
        qs = [s.sb(f"qs{b}", [P, LAT], F32R) for b in range(2)]
        kn = [s.pair(f"kn{b}", [P, T]) for b in range(2)]
        v = [s.pair(f"v{b}", [P, NT, DN]) for b in range(2)]
        wq_raw, wk_raw = s.sb("wq_raw", [P, 3, DN + DR]), s.sb("wk_raw", [P, 2, 2 * DN])
        wq, wk = s.pair("wq", [P, 3, DN + DR]), s.pair("wk", [P, 2, 2 * DN])
        prob = [s.sb(f"prob{x}", [P, T]) for x in range(2)]
        pt = s.pair("pt", [P, NT, 512])
        zg = [s.sb(f"zg{x}", [P, 512]) for x in range(2)]
        og = [s.sb(f"og{x}", [P, 512]) for x in range(2)]
        turn = [[s.sb(f"turn{j}{x}", [DR, 512]) for x in range(2)] for j in range(2)]
        top, bias, total, rec = ([s.sb(f"{n}{x}", [P, 1]) for x in range(2)] for n in ("top", "bias", "total", "rec"))
        S = [s.bank(f"scores{x}", 3) for x in range(2)]
        ring = [s.bank(f"ring{x}") for x in range(2)]
        wq_in, wk_in, wq_hi_ok, wk_hi_ok, wq_ok, wk_ok = (s.sem(n) for n in ("wq_in", "wk_in", "wq_hi_ok", "wk_hi_ok", "wq_ok", "wk_ok"))
        ring_done, ring_hi, ring_free = s.sem("ring_done"), s.sem("ring_hi"), s.sem("ring_free")
        qk_done, top_ok, bias_ok, exp_ok, rec_ok, prob_ok = (s.sem(n) for n in ("qk_done", "top_ok", "bias_ok", "exp_ok", "rec_ok", "prob_ok"))
        og_seen, turn_ok, qs_hi_ok, qs_ok = s.sem("og_seen"), s.sem("turn_ok"), s.sem("qs_hi_ok"), s.sem("qs_ok")
        zg_in, og_out = [s.sem(f"zg_in{x}") for x in range(2)], [s.sem(f"og_out{x}") for x in range(2)]
        wq_src = a["od_w_uq"].rearrange("a (k p) n -> p (a k) n", p=P)
        wk_src = a["od_w_ukv"].rearrange("a (k p) n -> p (a k) n", p=P)
        zg_src, og_dst = a["zgT"], a["ogT"]
        block = ctx.enter_context(nc.Block())

        def run(eng, prologue, slot, tail):
            prologue()
            for b in range(2):
                for t in range(QT):
                    slot("first", 0, b, t)
            with eng.Fori(1, AH // 2 - 1) as i:
                for b in range(2):
                    for t in range(QT):
                        slot("loop", i, b, t)
            for b in range(2):
                for t in range(QT):
                    slot("last", AH // 2 - 1, b, t)
            tail()

        def ring_ops(part, b, t):
            ops = slot_ops(t)
            if part == "first" and b == 0:
                ops = [[op for op in p if not (op == ("PV", 1) or (op[0] == "T" and t < 2))] for p in ops]
            if part == "last" and b == 1:
                ops = [[op for op in p if op[0] not in NEW] for p in ops]
            return ops

        head = lambda i, b, per, c=0: i * (2 * per) + (b * per + c)

        def place(op, nh, bank, half):
            kind = op[0]
            if kind == "qn":
                return qn[nh][half][:, 512 * op[1]:512 * op[1] + 512], bank[:, :]
            if kind == "kn":
                k0, n = KEYS[op[1]]
                return kn[nh][half][:, k0:k0 + n], bank[:, 0:n]
            c0, n = (VTILES if kind == "v" else KTILES)[op[-1]]
            view = bank[:, 0:n * P].rearrange("p (c e) -> p c e", e=P)
            if kind == "v":
                return v[nh][half][:, c0:c0 + n, :], view
            col = (op[1] % 4) * P
            return pt[half][:, c0:c0 + n, col:col + P], view

        @block.sync
        def _(sp):
            def weights(which, i, b, d):
                raw, src, n, ready, used = ((wq_raw, wq_src, DN + DR, wq_in, wq_ok), (wk_raw, wk_src, 2 * DN, wk_in, wk_ok))[which]
                col = i * (2 * n) + (b + d) * n
                if not isinstance(i, int):
                    col = sp.snap(col)
                if d:
                    sp.wait_ge(used, head(i, b, 1, d))
                sp.dma_start(raw[:, :, :], src[:, :, bass.ds(col, n)]).then_inc(ready, 16)

            def gates(row, x):
                sp.dma_start(zg[x][:, :], zg_src[bass.ds(row, P), 512 * x:512 * x + 512]).then_inc(zg_in[x], 16)

            def store(row, x):
                sp.dma_start(og_dst[bass.ds(row, P), 512 * x:512 * x + 512], og[x][:, :]).then_inc(og_out[x], 16)

            def slot(part, i, b, t):
                if t == 0 and part != "last":
                    weights(0, i, b, 2)
                    weights(1, i, b, 2)
                for op in [op for p in ring_ops(part, b, t) for op in p]:
                    if op[0] == "PV":
                        x = op[1]
                        row, nxt = i * (2 * P) + (b - x) * P, i * (2 * P) + (b - x + 1) * P
                        if not isinstance(i, int):
                            row, nxt = sp.snap(row), sp.snap(nxt)
                        sp.wait_ge(ring_free, order(part, i, b, op))
                        sp.sem_inc(og_seen, 1)
                        store(row, x)
                        if not (part == "last" and b == 1 and x == 0):
                            gates(nxt, x)

            def prologue():
                for d in range(2):
                    weights(0, 0, 0, d)
                    weights(1, 0, 0, d)
                gates(0, 0)
                gates(0, 1)

            def tail():
                sp.wait_ge(ring_free, order("tail", 0, 0, ("PV", 1)))
                store((AH - 1) * P, 1)
                for x in range(2):
                    sp.wait_ge(og_out[x], 16 * AH)
            run(sp, prologue, slot, tail)

        @block.gpsimd
        def _(pool):
            def turned(part, i, b, j):
                pool.wait_ge(ring_free, order(part, i, b, ("qr", j)))
                pool.tensor_tensor(turn[j][0][:, :], turn[j][0][:, :], turn[j][1][:, :], ALU.add).then_inc(turn_ok, 1)

            def slot(part, i, b, t):
                for op in [op for p in ring_ops(part, b, t) for op in p]:
                    if op[0] == "qr":
                        turned(part, i, b, op[1])

            def prologue():
                turned("prologue", 0, 0, 0)
                turned("prologue", 0, 0, 1)
            run(pool, prologue, slot, lambda: None)

        @block.scalar
        def _(act):
            def split_q(i, b, d):
                act.wait_ge(wq_in, head(i, b, 16, 16 * (d + 1)))
                nc.scalar.copy(wq[0][:, :, :], wq_raw[:, :, :]).then_inc(wq_hi_ok, 1)

            def split_k(i, b, d):
                act.wait_ge(wk_in, head(i, b, 16, 16 * (d + 1)))
                nc.scalar.copy(wk[0][:, :, :], wk_raw[:, :, :]).then_inc(wk_hi_ok, 1)

            def high(part, i, b, op):
                if not has_hi(op):
                    return
                n = order(part, i, b, op)
                bank = ring[order(part, 0 if part == "loop" else i, b, op) % 2]
                nh = 0 if part == "prologue" else 1 - b
                act.wait_ge(ring_done, n)
                dst, src = place(op, nh, bank, 0)
                nc.scalar.copy(dst, src).then_inc(ring_hi, 1)

            def turned_high(i, b, d, nh):
                for j in range(2):
                    act.wait_ge(turn_ok, head(i, b, 2, 2 * d + j + 1))
                    nc.scalar.copy(qs[nh][0:DR, 512 * j:512 * j + 512], turn[j][0][:, :]).then_inc(qs_hi_ok, 1)

            def exponentials(i, b, t):
                x = t % 2
                act.wait_ge(bias_ok, head(i, b, QT, t + 1))
                nc.scalar.activation(prob[x][:, :], S[x][:, 0:T], ACT.Exp, scale=ATT_SCALE, bias=bias[x][:, :],
                                     accum_out=total[x][:, :]).then_inc(exp_ok, 1)

            def slot(part, i, b, t):
                ops = ring_ops(part, b, t)
                more = not (part == "last" and b == 1)
                before = not (part == "first" and b == 0 and t == 0)
                for op in ops[0]:
                    high(part, i, b, op)
                for op in ops[1]:
                    high(part, i, b, op)
                    if op[0] == "T" and before:
                        exponentials(i, b, t - 1)
                    if t == QS_SLOT and more and op == ("T", 0, 1):
                        turned_high(i, b, 1, 1 - b)
                if before and not any(op[0] == "T" for op in ops[1]):
                    exponentials(i, b, t - 1)
                for op in ops[2]:
                    high(part, i, b, op)
                if part != "last":
                    if t == WQ_SLOT:
                        split_q(i, b, 2)
                    if t == WK_SLOT:
                        split_k(i, b, 2)

            def prologue():
                split_q(0, 0, 0)
                split_k(0, 0, 0)
                for op in PROLOGUE:
                    high("prologue", 0, 0, op)
                turned_high(0, 0, 0, 0)
                act.wait_ge(ring_done, len(PROLOGUE))
                split_q(0, 0, 1)
                split_k(0, 0, 1)

            def tail():
                for op in TAIL:
                    high("tail", 0, 1, op)
                    if op == ("T", 6, 0):
                        exponentials(AH // 2 - 1, 1, QT - 1)
            run(act, prologue, slot, tail)

        @block.vector
        def _(dve):
            def low(part, i, b, op):
                n = order(part, i, b, op)
                bank = ring[order(part, 0 if part == "loop" else i, b, op) % 2]
                nh = 0 if part == "prologue" else 1 - b
                if has_hi(op):
                    dve.wait_ge(ring_hi, order(part, i, b, op, has_hi))
                    dst, src = place(op, nh, bank, 1)
                    hi = place(op, nh, bank, 0)[0]
                    nc.vector.tensor_tensor(dst, src, f(hi), ALU.subtract).then_inc(ring_free, 1)
                elif op[0] == "qr":
                    dve.wait_ge(ring_done, n)
                    j, HR = op[1], DR // 2
                    cols = slice(512 * j, 512 * j + 512)
                    nc.vector.tensor_tensor(turn[j][0][:, :], bank[0:DR, :], rope[:, 0, cols], ALU.mult)
                    nc.vector.tensor_tensor(turn[j][1][HR:DR, :], bank[0:HR, :], rope[0:HR, 1, cols], ALU.mult)
                    nc.vector.tensor_tensor(turn[j][1][0:HR, :], bank[HR:DR, :], rope[HR:DR, 1, cols], ALU.mult).then_inc(ring_free, 1)
                else:
                    x = op[1]
                    dve.wait_ge(ring_done, n)
                    if part == "tail":
                        dve.wait_ge(zg_in[x], 16 * AH)
                        dve.wait_ge(og_out[x], 16 * (AH - 1))
                    else:
                        dve.wait_ge(zg_in[x], head(i, b, 16, 16 * (1 - x)))
                        if not (part == "first" and b - x == 0):
                            dve.wait_ge(og_out[x], head(i, b, 16, -16 * x))
                    nc.vector.scalar_tensor_tensor(og[x][:, :], bank[:, :], 0.5, zg[x][:, :], ALU.mult, ALU.mult).then_inc(ring_free, 1)

            def normalise(i, b, t):
                x = t % 2
                dve.wait_ge(exp_ok, head(i, b, QT, t + 1))
                nc.vector.reciprocal(rec[x][:, :], total[x][:, :]).then_inc(rec_ok, 1)
                dve.wait_ge(rec_ok, head(i, b, QT, t + 1))
                nc.vector.tensor_scalar(prob[x][:, :], prob[x][:, :], rec[x][:, :], None, ALU.mult).then_inc(prob_ok, 1)

            def maximum(i, b, t):
                x = t % 2
                dve.wait_ge(qk_done, head(i, b, QT, t + 1))
                nc.vector.reduce_max(top[x][:, :], S[x][:, 0:T], axis=AX).then_inc(top_ok, 1)
                dve.wait_ge(top_ok, head(i, b, QT, t + 1))
                nc.vector.tensor_scalar(bias[x][:, :], top[x][:, :], -ATT_SCALE, None, ALU.mult).then_inc(bias_ok, 1)

            def split_q(i, b, d):
                dve.wait_ge(wq_hi_ok, head(i, b, 1, d + 1))
                nc.vector.tensor_tensor(wq[1][:, :, :], wq_raw[:, :, :], f(wq[0][:, :, :]), ALU.subtract).then_inc(wq_ok, 1)

            def split_k(i, b, d):
                dve.wait_ge(wk_hi_ok, head(i, b, 1, d + 1))
                nc.vector.tensor_tensor(wk[1][:, :, :], wk_raw[:, :, :], f(wk[0][:, :, :]), ALU.subtract).then_inc(wk_ok, 1)

            def turned_low(i, b, d, nh):
                for j in range(2):
                    cols = slice(512 * j, 512 * j + 512)
                    dve.wait_ge(qs_hi_ok, head(i, b, 2, 2 * d + j + 1))
                    nc.vector.tensor_tensor(qs[nh][DR:P, cols], turn[j][0][:, :], f(qs[nh][0:DR, cols]), ALU.subtract).then_inc(qs_ok, 1)

            def slot(part, i, b, t):
                ops = ring_ops(part, b, t)
                more = not (part == "last" and b == 1)
                before = not (part == "first" and b == 0 and t == 0)
                if before:
                    maximum(i, b, t - 1)
                for op in ops[0]:
                    low(part, i, b, op)
                for op in ops[1]:
                    low(part, i, b, op)
                    if op[0] == "T" and before:
                        normalise(i, b, t - 1)
                    if t == QS_SLOT and more and op == ("T", 0, 1):
                        turned_low(i, b, 1, 1 - b)
                if before and not any(op[0] == "T" for op in ops[1]):
                    normalise(i, b, t - 1)
                for op in ops[2]:
                    low(part, i, b, op)
                if part != "last":
                    if t == WQ_SLOT:
                        split_q(i, b, 2)
                    if t == WK_SLOT:
                        split_k(i, b, 2)

            def prologue():
                split_q(0, 0, 0)
                split_k(0, 0, 0)
                for op in PROLOGUE:
                    low("prologue", 0, 0, op)
                turned_low(0, 0, 0, 0)
                split_q(0, 0, 1)
                split_k(0, 0, 1)

            def tail():
                maximum(AH // 2 - 1, 1, QT - 1)
                for op in TAIL:
                    low("tail", 0, 1, op)
                    if op == ("T", 6, 0):
                        normalise(AH // 2 - 1, 1, QT - 1)
            run(dve, prologue, slot, tail)

        @block.tensor
        def _(pe):
            def project(op, bank):
                kind, j = op
                if kind in ("qn", "qr"):
                    cols = slice(0, DN) if kind == "qn" else slice(DN, DN + DR)
                    for k in range(3):
                        last = mm3(nc, bank[0:cols.stop - cols.start, :], (wq[0][:, k, cols], wq[1][:, k, cols]),
                                   (lq[0][:, k, 512 * j:512 * j + 512], lq[1][:, k, 512 * j:512 * j + 512]), k == 0, k == 2)
                elif kind == "kn":
                    k0, n = KEYS[j]
                    for k in range(2):
                        last = mm3(nc, bank[:, 0:n], (wk[0][:, k, 0:DN], wk[1][:, k, 0:DN]),
                                   (lkv[0][:, k, k0:k0 + n], lkv[1][:, k, k0:k0 + n]), k == 0, k == 1)
                else:
                    c0, n = VTILES[j]
                    for c in range(n):
                        tok = slice((c0 + c) * P, (c0 + c + 1) * P)
                        for k in range(2):
                            last = mm3(nc, bank[:, c * P:(c + 1) * P], (lkv[0][:, k, tok], lkv[1][:, k, tok]),
                                       (wk[0][:, k, DN:2 * DN], wk[1][:, k, DN:2 * DN]), k == 0, k == 1)
                return last

            def ring_op(part, i, b, op):
                n = order(part, i, b, op)
                bank = ring[order(part, 0 if part == "loop" else i, b, op) % 2]
                if not (part == "prologue" and n <= 2):
                    pe.wait_ge(ring_free, order(part, i, b, op, c=-2))
                if op[0] in NEW:
                    if op in (("qn", 0), ("kn", 0)):
                        w_ok = wq_ok if op[0] == "qn" else wk_ok
                        pe.wait_ge(w_ok, 1 if part == "prologue" else head(i, b, 1, 2))
                    last = project(op, bank)
                elif op[0] == "T":
                    _, t, g = op
                    old = part == "tail" or op in OLD
                    if g == 0:
                        pe.wait_ge(prob_ok, AH * QT - QT + t + 1 if part == "tail" else head(i, b, QT, t + 1 - (QT if old else 0)))
                    c0, m = KTILES[g]
                    for c in range(m):
                        last = nc.tensor.transpose(bank[:, c * P:(c + 1) * P], prob[t % 2][:, (c0 + c) * P:(c0 + c + 1) * P], ident[:, :])
                else:
                    x = op[1]
                    tile = ("T", 4 * x + 3, 2)
                    if part == "tail":
                        m, vb = order("tail", 0, 1, tile), 1
                    else:
                        m, vb = order(part, i, b, tile), (b if x == 0 else 1 - b)
                    pe.wait_ge(ring_free, m)
                    for c in range(NT):
                        last = mm3(nc, bank[:, :], (v[vb][0][:, c, :], v[vb][1][:, c, :]), (pt[0][:, c, :], pt[1][:, c, :]), c == 0, c == NT - 1)
                last.then_inc(ring_done, 1)

            def scores(b, t, j):
                k0, n = KEYS[j]
                out, tok = S[t % 2][:, k0:k0 + n], slice(t * P, (t + 1) * P)
                mm3(nc, out, (qn[b][0][:, tok], qn[b][1][:, tok]), (kn[b][0][:, k0:k0 + n], kn[b][1][:, k0:k0 + n]), True, False)
                nc.tensor.matmul(out, qs[b][:, tok], kr2[0][:, k0:k0 + n], start=False, stop=False)
                return nc.tensor.matmul(out, qs[b][:, tok], kr2[1][:, k0:k0 + n], start=False, stop=True)

            def slot(part, i, b, t):
                if t == 0:
                    pe.wait_ge(qs_ok, head(i, b, 2, 2))
                    if part == "first" and b == 0:
                        pe.wait_ge(ring_free, len(PROLOGUE))
                    else:
                        pe.wait_ge(ring_free, order(part, i, b, ("T", 6, 0), c=-(len(SEQ) - SEQ.index(("kn", 2)))))
                if not (part == "first" and b == 0 and t < 2):
                    pe.wait_ge(exp_ok, head(i, b, QT, t - 1))
                ops = ring_ops(part, b, t)
                for j in range(3):
                    last = scores(b, t, j)
                    if j == 2:
                        last.then_inc(qk_done, 1)
                    for op in ops[j]:
                        ring_op(part, i, b, op)

            def prologue():
                for op in PROLOGUE:
                    ring_op("prologue", 0, 0, op)

            def tail():
                for op in TAIL:
                    ring_op("tail", 0, 1, op)
            run(pe, prologue, slot, tail)


def constants():
    sel = np.array([[1, 0], [0, 1], [1, 0], [0, 1], [1, 1]], np.float32)
    s, t = np.meshgrid(np.arange(P), np.arange(P), indexing="ij")
    mask = np.stack([np.where(s <= t, 0, NEG), np.where(s >= t, 0, NEG)]).astype(np.float32)
    tok = np.arange(LAT)
    freq = np.float32(10000.0) ** (-np.arange(DR // 4, dtype=np.float32) / np.float32(DR // 4))
    ang = np.concatenate([(tok // 64)[None, :] * freq[:, None], (tok % 64)[None, :] * freq[:, None]]).astype(np.float32)
    cos, sin = np.cos(ang), np.sin(ang)
    rope = np.stack([np.concatenate([cos, cos]), np.concatenate([sin, -sin])]).astype(np.float32)
    return {"c_ident": np.eye(P, dtype=np.float32), "c_sel": sel, "c_mask": mask, "c_rope": rope}


def layout(inputs):
    arrays = {n: np.ascontiguousarray(x) for n, x in inputs.items() if n not in ("x", "ctx", "ev_conv_w")}
    arrays["conv_t"] = np.ascontiguousarray(np.asarray(inputs["ev_conv_w"])[0].T)
    arrays["h0"] = np.concatenate([np.asarray(inputs["ctx"])[0], np.asarray(inputs["x"])[0]])
    for n in ("od_q_norm", "od_kv_norm"):
        arrays[n] = np.ascontiguousarray(arrays[n].reshape(-1, P).T)
    arrays.update(constants())
    return arrays


def build(nc, a):
    with ExitStack() as ctx:
        s = Space(nc, ctx, "k")
        keep = {
            "ident": s.sb("ident", [P, P]),
            "mod_col": s.sb("mod_col", [P, 2, 24, 2]),
        }
        for name, shape in (("g_rows", (2, 2, D)), ("mixT", (MIX, T)), ("h1", (LAT, D)), ("u1T", (D, T)), ("zgT", (MIX, LAT)), ("ogT", (MIX, LAT))):
            a[name] = nc.dram_tensor(name, shape, F32).ap()
        with ExitStack() as even:
            se = Space(nc, even, "e")
            keep["u_hi"], keep["u_lo"] = se.pair("u", [P, KD, T])
            keep["gate_col"] = se.sb("gate_col", [P, 6, NT, 8])
            stage_modulate(nc, a, keep)
            stage_gates(nc, a, keep)
            stage_even(nc, a, keep)
        stage_out(nc, a, keep, 0)
        with ExitStack() as odd:
            sa = Space(nc, odd, "a")
            keep["lq"], keep["lkv"], keep["kr2"] = sa.pair("lq", [P, 3, LAT]), sa.pair("lkv", [P, 2, T]), sa.pair("kr2", [P, T])
            keep["rope"] = sa.sb("rope", [DR, 2, LAT])
            stage_latent(nc, a, keep)
            stage_attend(nc, a, keep)
        stage_out(nc, a, keep, 1)


def kernel(**inputs):
    import concourse.bacc as bacc
    from concourse.bass_utils import run_bass_kernel_spmd

    nc = bacc.Bacc("TRN2", target_bir_lowering=False, num_devices=1)
    arrays = layout(inputs)
    a = {n: nc.dram_tensor("in_" + n, x.shape, mybir.dt.from_np(x.dtype), kind="ExternalInput").ap() for n, x in arrays.items()}
    a["out"] = nc.dram_tensor("out", (LAT, D), F32, kind="ExternalOutput").ap()
    build(nc, a)
    r = run_bass_kernel_spmd(nc, [{"in_" + n: x for n, x in arrays.items()}], core_ids=[0])
    return r.results[0]["out"].reshape(1, LAT, D)
```
